# Optimizing a Trainium2 kernel written in Bass

```python
import math
import jax, jax.numpy as jnp
from jax import lax
import numpy as np

D_MODEL = 1024
BATCH = 1
SEQ = 2048
DEPTH = 1

D_MIX = 2 * D_MODEL
GROUP_W = D_MIX // 4
HEAD_DIM = 64
N_HEADS_DIFF = GROUP_W // (2 * HEAD_DIM)
DIFF_V_DIM = 2 * HEAD_DIM
N_HEADS_SB = GROUP_W // HEAD_DIM
N_HEADS_FOX = GROUP_W // HEAD_DIM
N_HEADS_MEM = 4
MEM_HEAD_DIM = GROUP_W // N_HEADS_MEM
MEM_LEN = 256
NUM_BUCKETS = 32
MAX_DISTANCE = 128
BLOCK_Q = 128
EPS = 1e-6
NEG = -1e30
COL_SIZES = (GROUP_W, GROUP_W, GROUP_W, GROUP_W, GROUP_W, GROUP_W, GROUP_W, GROUP_W, GROUP_W, N_HEADS_FOX, GROUP_W, D_MIX)
D_IN_PROJ = sum(COL_SIZES)
COL_SPLITS = tuple(int(c) for c in np.cumsum(COL_SIZES)[:-1])

kernel_name = 'hybrid_diff_stickbreak_fox_mem_block'

def _rmsnorm(x, g):
    x32 = x.astype(jnp.float32)
    y = x32 * lax.rsqrt(jnp.mean(x32 * x32, axis=-1, keepdims=True) + EPS)
    return y.astype(x.dtype) * g

def _heads(t, n):
    b, s, _ = t.shape
    return t.reshape(b, s, n, -1).transpose(0, 2, 1, 3)

def _merge(t):
    b, h, s, d = t.shape
    return t.transpose(0, 2, 1, 3).reshape(b, s, h * d)

def _to_blocks(t):
    b, h, s = t.shape[:3]
    t = t.reshape((b, h, s // BLOCK_Q, BLOCK_Q) + t.shape[3:])
    return jnp.moveaxis(t, 2, 0)

def _from_blocks(t):
    nb, b, h, bq, d = t.shape
    return jnp.moveaxis(t, 0, 2).reshape(b, h, nb * bq, d)

def _block_dist(i, s):
    q_pos = i * BLOCK_Q + jnp.arange(BLOCK_Q, dtype=jnp.int32)
    k_pos = jnp.arange(s, dtype=jnp.int32)
    return q_pos[:, None] - k_pos[None, :]

def _t5_bucket(n):
    max_exact = NUM_BUCKETS // 2
    nf = jnp.maximum(n, 1).astype(jnp.float32)
    large = max_exact + (jnp.log(nf / max_exact) / math.log(MAX_DISTANCE / max_exact)
                         * (NUM_BUCKETS - max_exact)).astype(jnp.int32)
    large = jnp.minimum(large, NUM_BUCKETS - 1)
    return jnp.where(n < max_exact, n, large)

def _diff_attention(q, k, v, rel_bias, lam):
    s = q.shape[2]
    scale = HEAD_DIM ** -0.5
    v32 = v.astype(jnp.float32)

    def block(args):
        i, qb = args
        dist = _block_dist(i, s)
        bias = rel_bias[_t5_bucket(jnp.maximum(dist, 0))]
        bias = jnp.moveaxis(bias, -1, 0).astype(jnp.float32)
        logits = jnp.einsum('bhqcd,bhkcd->bchqk', qb, k).astype(jnp.float32) * scale + bias
        logits = jnp.where(dist >= 0, logits, NEG)
        p = jax.nn.softmax(logits, axis=-1)
        a = p[:, 0] - lam * p[:, 1]
        return jnp.einsum('bhqk,bhkd->bhqd', a, v32)

    out = lax.map(block, (jnp.arange(s // BLOCK_Q), _to_blocks(q)))
    return _from_blocks(out)

def _stick_breaking(q, k, v):
    s = q.shape[2]
    scale = HEAD_DIM ** -0.5
    v32 = v.astype(jnp.float32)

    def block(args):
        i, qb = args
        strict = _block_dist(i, s) > 0
        z = jnp.einsum('bhqd,bhkd->bhqk', qb, k).astype(jnp.float32) * scale
        log_rest = jnp.where(strict, jax.nn.log_sigmoid(-z), 0.0)
        tail = lax.cumsum(log_rest, axis=3, reverse=True) - log_rest
        log_a = jax.nn.log_sigmoid(z) + tail
        a = jnp.where(strict, jnp.exp(log_a), 0.0)
        return jnp.einsum('bhqk,bhkd->bhqd', a, v32)

    out = lax.map(block, (jnp.arange(s // BLOCK_Q), _to_blocks(q)))
    return _from_blocks(out)

def _forgetting_attention(q, k, v, log_f):
    s = q.shape[2]
    scale = HEAD_DIM ** -0.5
    v32 = v.astype(jnp.float32)
    c = jnp.cumsum(log_f, axis=-1)

    def block(args):
        i, qb, cb = args
        dist = _block_dist(i, s)
        logits = jnp.einsum('bhqd,bhkd->bhqk', qb, k).astype(jnp.float32) * scale
        logits = logits + (cb[..., :, None] - c[..., None, :])
        logits = jnp.where(dist >= 0, logits, NEG)
        p = jax.nn.softmax(logits, axis=-1)
        return jnp.einsum('bhqk,bhkd->bhqd', p, v32)

    out = lax.map(block, (jnp.arange(s // BLOCK_Q), _to_blocks(q), _to_blocks(c)))
    return _from_blocks(out)

def _memory_attention(q, km, vm):
    scale = MEM_HEAD_DIM ** -0.5
    logits = jnp.einsum('bhqd,bhkd->bhqk', q, km).astype(jnp.float32) * scale
    p = jax.nn.softmax(logits, axis=-1)
    return jnp.einsum('bhqk,bhkd->bhqd', p, vm.astype(jnp.float32))

def setup_inputs(seed: int = 0) -> dict:
    key = jax.random.key(seed)
    ks = jax.random.split(key, 12)
    f32 = jnp.float32
    x = jax.random.normal(ks[0], (BATCH, SEQ, D_MODEL), f32)
    mem = jax.random.normal(ks[1], (BATCH, MEM_LEN, D_MODEL), f32)
    w_in = jax.random.normal(ks[2], (DEPTH, D_MODEL, D_IN_PROJ), f32) * D_MODEL ** -0.5
    b_forget = jax.random.uniform(ks[3], (DEPTH, N_HEADS_FOX), f32, minval=1.0, maxval=4.0)
    w_mem_kv = jax.random.normal(ks[4], (DEPTH, D_MODEL, 2 * GROUP_W), f32) * D_MODEL ** -0.5
    w_out = jax.random.normal(ks[5], (DEPTH, D_MIX, D_MODEL), f32) * D_MIX ** -0.5
    pre_norm = 1.0 + 0.05 * jax.random.normal(ks[6], (DEPTH, D_MODEL), f32)
    post_norm = 1.0 + 0.05 * jax.random.normal(ks[7], (DEPTH, D_MODEL), f32)
    mem_norm = 1.0 + 0.05 * jax.random.normal(ks[8], (DEPTH, D_MODEL), f32)
    diff_lambda = 0.1 * jax.random.normal(ks[9], (DEPTH, 4, HEAD_DIM), f32)
    diff_head_norm = 1.0 + 0.05 * jax.random.normal(ks[10], (DEPTH, DIFF_V_DIM), f32)
    rel_bias = 0.5 * jax.random.normal(ks[11], (NUM_BUCKETS, N_HEADS_DIFF), f32)
    return {'x': x, 'mem': mem, 'w_in': w_in, 'b_forget': b_forget, 'w_mem_kv': w_mem_kv,
            'w_out': w_out, 'pre_norm': pre_norm, 'post_norm': post_norm, 'mem_norm': mem_norm,
            'diff_lambda': diff_lambda, 'diff_head_norm': diff_head_norm, 'rel_bias': rel_bias}

def reference(x, mem, w_in, b_forget, w_mem_kv, w_out, pre_norm, post_norm, mem_norm,
              diff_lambda, diff_head_norm, rel_bias):
    dt = x.dtype
    b, s, _ = x.shape
    for l in range(DEPTH):
        h = _rmsnorm(x, pre_norm[l])
        proj = h @ w_in[l]
        (a_q, a_k, a_v, sb_q, sb_k, sb_v, f_q, f_k, f_v, f_logit, m_q, gate) = jnp.split(
            proj, COL_SPLITS, axis=-1)

        lam_init = 0.8 - 0.6 * math.exp(-0.3 * l)
        lam_p = diff_lambda[l].astype(jnp.float32)
        lam = (jnp.exp(jnp.sum(lam_p[0] * lam_p[1])) - jnp.exp(jnp.sum(lam_p[2] * lam_p[3]))
               + lam_init)
        qa = _heads(a_q, N_HEADS_DIFF).reshape(b, N_HEADS_DIFF, s, 2, HEAD_DIM)
        ka = _heads(a_k, N_HEADS_DIFF).reshape(b, N_HEADS_DIFF, s, 2, HEAD_DIM)
        va = _heads(a_v, N_HEADS_DIFF)
        o_a = _diff_attention(qa, ka, va, rel_bias, lam)
        o_a = _rmsnorm(o_a, diff_head_norm[l]) * (1.0 - lam_init)

        o_b = _stick_breaking(_heads(sb_q, N_HEADS_SB), _heads(sb_k, N_HEADS_SB),
                              _heads(sb_v, N_HEADS_SB))

        log_f = jax.nn.log_sigmoid((f_logit + b_forget[l]).astype(jnp.float32)).transpose(0, 2, 1)
        o_c = _forgetting_attention(_heads(f_q, N_HEADS_FOX), _heads(f_k, N_HEADS_FOX),
                                    _heads(f_v, N_HEADS_FOX), log_f)

        kv = _rmsnorm(mem, mem_norm[l]) @ w_mem_kv[l]
        km, vm = jnp.split(kv, 2, axis=-1)
        o_m = _memory_attention(_heads(m_q, N_HEADS_MEM), _heads(km, N_HEADS_MEM),
                                _heads(vm, N_HEADS_MEM))

        y = jnp.concatenate([_merge(o_a).astype(dt), _merge(o_b).astype(dt),
                             _merge(o_c).astype(dt), _merge(o_m).astype(dt)], axis=-1)
        y = y * jax.nn.silu(gate)
        x = x + _rmsnorm(y @ w_out[l], post_norm[l])
    return x


_drawn_inputs = setup_inputs


def setup_inputs(seed=0):
    import zlib

    import numpy as np

    out = dict(_drawn_inputs(seed))
    spreads = {}
    factors = {'mem_norm': 8.0, 'diff_lambda': 4.915, 'b_forget': 2.778, 'diff_head_norm': 8.0}
    for name, (base, spread) in spreads.items():
        noise = np.random.default_rng([zlib.crc32(name.encode()), seed]).standard_normal(out[name].shape)
        drawn = base * np.exp(spread * noise) if base else spread * noise
        out[name] = __import__('jax').numpy.asarray(drawn.astype(out[name].dtype))
    for name, factor in factors.items():
        out[name] = (out[name] * factor).astype(out[name].dtype)
    return out
```

```python
from contextlib import ExitStack

import concourse.bass as bass
import numpy as np
from concourse import mybir

ALU = mybir.AluOpType
ACT = mybir.ActivationFunctionType
AX_X = mybir.AxisListType.X
F32 = mybir.dt.float32
F16 = mybir.dt.float16
BF16 = mybir.dt.bfloat16

P = 128
HEAD_DIM = 64
GROUP_W = 512
PAIR_W = 128
UNITS = GROUP_W // PAIR_W
BUCKETS = 32
MAX_DISTANCE = 128
EPS = 1e-6
NEG = -1e30
LAM_INIT = 0.2
W_SCALE = 64.0
GATE_MIN = -41.0
BANK = 512
LATE_PROBS, LATE_DIFF, B_START, B_DIFF, MIX_LAG, P0_LAG, SILU = 0.2, 0.02, 0.1, 0.1, 2, 1, 0.2
S_BANKS, T_BANKS, J_BANKS, PT_RING, ROWS = 3, 2, 2, 4, 4
Q, K, V, G = range(4)
HK, HQ, LQ, LK = range(4)

COL_FORGET = 9 * GROUP_W
HEADS_FOX = GROUP_W // HEAD_DIM
COL_MEM = COL_FORGET + HEADS_FOX
COL_GATE = COL_MEM + GROUP_W


class Unit:

    def __init__(self, kind, group, slot, scale):
        self.kind, self.group, self.slot, self.scale = kind, group, slot, scale
        base = 3 * GROUP_W * group
        self.col = {Q: base, K: base + GROUP_W, V: base + 2 * GROUP_W, G: COL_GATE + GROUP_W * group}
        if kind == "mem":
            self.col[Q] = COL_MEM
        self.has_k = kind != "mem"


UNIT = [
    Unit("mem", 3, 1, float(PAIR_W) ** -0.5),
    Unit("stick", 1, 0, HEAD_DIM ** -0.5),
    Unit("forget", 2, 1, HEAD_DIM ** -0.5),
    Unit("diff", 0, 0, HEAD_DIM ** -0.5),
]


def distance_tables(width):
    dist = np.arange(width) - (P - 1)
    n = np.maximum(dist, 0)
    exact = BUCKETS // 2
    big = np.log(np.maximum(n, 1) / exact) / np.log(MAX_DISTANCE / exact) * (BUCKETS - exact)
    bucket = np.where(n < exact, n, np.minimum(exact + big.astype(np.int64), BUCKETS - 1))
    pick = (np.arange(BUCKETS)[:, None] == bucket[None, :]).astype(np.float32)
    pick[BUCKETS - 1] -= 1.0
    mask = np.where(dist < 0, np.float32(NEG), np.float32(0.0))[None, :].repeat(UNITS, 0)
    return pick, np.ascontiguousarray(mask.astype(np.float32))


class Plan:

    def __init__(self, seq, k_tiles):
        self.nt = nt = seq // P
        self.k_tiles = k_tiles
        self.steps = [(t, i) for t in range(len(UNIT)) for i in range(nt)]
        self.n_steps = len(self.steps)
        self.chunks, self.t_chunks, self.last_chunk = {}, {}, {}
        self.first_chunk, self.row_index = {}, {}
        n = tau = 0
        for g, (t, i) in enumerate(self.steps):
            kind = UNIT[t].kind
            self.first_chunk.setdefault(t, n)
            keys = 2 * P if kind == "mem" else (i + 1) * P
            cuts = [(c, min(BANK, keys - c)) for c in range(0, keys, BANK)]
            if kind == "stick":
                cuts.reverse()
            self.chunks[g] = []
            for m in range(2 if UNIT[t].has_k else 1):
                self.row_index[g, m] = len(self.row_index)
                for c, w in cuts:
                    self.chunks[g].append((n, m, c, w))
                    n += 1
            self.last_chunk[t] = n
            self.t_chunks[g] = []
            for m in range(2 if kind in ("stick", "forget") else 1):
                for k in range(0, keys // P, BANK // P):
                    self.t_chunks[g].append((tau, m, k, min(BANK // P, keys // P - k)))
                    tau += 1
        self.n_chunks, self.n_tau = n, tau
        self.j = self.c = 0
        self.conv_of, self.gate_job, self.y_job, self.qk_jobs = {}, {}, {}, {}
        self.script = [("convert", self.conv(0, Q))]
        for c in range(seq // BANK):
            self.script += [op for _, op in self.project("qk", 0, Q, c)]
        for p in range(self.n_steps + 2):
            self.script += self.position(p)
        self.n_jobs, self.n_convs = self.j, self.c

    def conv(self, t, kind):
        self.conv_of[t, kind] = self.c
        self.c += 1
        return self.c - 1, t, kind

    def job(self, what, t, kind, index):
        self.j += 1
        j = (self.j - 1, what, t, kind, index)
        if what == "qk":
            self.qk_jobs[t, index] = j[0]
        return j

    def project(self, what, t, kind, index):
        j = self.job(what, t, kind, index)
        step = 1 if what == "qk" else self.k_tiles // 2
        ops = [(0.7, ("part", j, k, k + step)) for k in range(0, self.k_tiles, step)]
        return ops if what == "g" else ops + [(0.0, ("halves", j))]

    def position(self, p):
        placed = []

        def spread(ops, low, high):
            total, at = sum(cost for cost, _ in ops) or 1.0, 0.0
            for cost, op in ops:
                placed.append((low + (high - low) * (at + cost / 2) / total, len(placed), op))
                at += cost

        g = p - 2
        if g >= 0:
            placed.append((0.02, 0, ("take", g)))
            if UNIT[self.steps[g][0]].kind == "diff":
                placed += [(0.06, 0, ("variance", g)), (0.10, 0, ("root", g))]
            placed.append((0.14, 0, ("post", g)))
        g = p - 1
        if 0 <= g < self.n_steps:
            t, i = self.steps[g]
            late = LATE_DIFF if UNIT[t].kind == "diff" else LATE_PROBS
            placed.append((late, 0, ("probs", g, self.chunks[g][-1][1])))
            ops, todo = [], self.t_chunks[g]
            if UNIT[t].kind == "diff":
                ops.append((0.3, ("combine", g, todo[0])))
            for q in range(len(todo) + MIX_LAG):
                if q < len(todo):
                    if UNIT[t].kind == "diff" and q + 1 < len(todo):
                        ops.append((0.3, ("combine", g, todo[q + 1])))
                    ops.append((0.13 * todo[q][3], ("turn", g, todo[q])))
                if q >= MIX_LAG:
                    r = q - MIX_LAG
                    ops.append((0.15 * todo[r][3], ("mix", g, todo[r], r == 0, r == len(todo) - 1)))
            spread(ops, B_DIFF if UNIT[t].kind == "diff" else B_START, 1.0)
        ops = []
        if 0 <= g < self.n_steps:
            ops = self.project("g", None, G, g)
            self.gate_job[g] = ops[0][1][1]
            spread(ops, 0.0, 0.2)
            placed += [(0.2, 1, ("gate", g)), (0.24 + SILU, 0, ("silu", g))]
            ops = []
        if p < self.n_steps:
            t, i = self.steps[p]
            if i == 0:
                placed.append((0.3, 0, ("convert", self.conv(t, G))))
            if t + 1 < len(UNIT):
                for at, kind in enumerate((V, Q, K)):
                    if i == at:
                        placed.append((0.31, 0, ("convert", self.conv(t + 1, kind))))
                v_tiles = [] if i == 0 else [i - 1]
                if i == self.nt - 1:
                    v_tiles.append(i)
                for v in v_tiles:
                    ops += self.project("v", t + 1, V, v)
                wide = [(kind, c) for c in range(self.nt * P // BANK) for kind in (Q, K)]
                for q, (kind, c) in enumerate(wide):
                    if i == min(3, self.nt - 1) + q * max(self.nt - 3, 0) // len(wide):
                        ops += self.project("qk", t + 1, kind, c)
        spread(ops, 0.25, 0.93)
        if p >= 2:
            self.y_job[p - 2] = self.job("y", None, None, p - 2)
            placed.append((0.95, 0, ("y", p - 2)))
        if p < self.n_steps:
            ops, stick = [], UNIT[self.steps[p][0]].kind == "stick"
            todo = self.chunks[p]
            rest = []
            for q in range(len(todo) + 1):
                if q < len(todo):
                    ops.append((0.1 + todo[q][3] / 1000, ("scores", p, todo[q])))
                if stick and q:
                    ops.append((todo[q - 1][3] / 1000, ("log", p, todo[q - 1])))
                if 2 * q == len(todo) + 2 * min(P0_LAG, len(todo) // 2) and len(todo) > 1:
                    ops.append((0.0, ("probs", p, 0)))
            spread(ops, *((1.0, 2.0) if self.steps[p][1] == 0 else (0.0, 1.0)))
        return [op for _, _, op in sorted(placed, key=lambda entry: entry[0])]


def build(nc, x, mem, w_in, b_forget, w_mem_kv, w_out, pre_norm, post_norm, mem_norm,
          diff_lambda, diff_head_norm, rel_bias, pick, dmask, out):
    _, SEQ, D = x.shape
    KT = D // P
    NT = SEQ // P
    NC = SEQ // BANK
    D_MIX = w_out.shape[1]
    YT = D_MIX // P
    MEM_T = mem.shape[1] // P
    MEM_LEN = mem.shape[1]
    DIST_W = pick.shape[1]
    plan = Plan(SEQ, KT)
    assert D == KT * P and MEM_T == 2 and KT * P <= 1024

    y_dram = nc.dram_tensor("y_halves", (2, D_MIX, SEQ), F16, kind="Internal").ap()
    c_dram = nc.dram_tensor("forget_parts", (3, HEADS_FOX, SEQ), BF16, kind="Internal").ap()
    dist_dram = nc.dram_tensor("bias_by_distance", (UNITS, DIST_W), F32, kind="Internal").ap()
    near_dram = nc.dram_tensor("near_bias", (UNITS, P, 2 * P), F32, kind="Internal").ap()
    km_dram = nc.dram_tensor("mem_keys", (UNITS, P, 2, MEM_LEN), F16, kind="Internal").ap()
    vm_dram = nc.dram_tensor("mem_values", (MEM_T, UNITS, P, 2, P), F16, kind="Internal").ap()

    w_cols = w_in[0].rearrange("(k p) n -> p k n", p=P)
    w_mem_cols = w_mem_kv[0].rearrange("(k p) n -> p k n", p=P)
    w_out_rows = w_out[0].rearrange("(k p) n -> k p n", p=P)

    with ExitStack() as ctx:
        def sb(name, shape, dt):
            return ctx.enter_context(nc.sbuf_tensor(name, shape, dt))

        def sem(name):
            return ctx.enter_context(nc.semaphore(name))

        s_bank = [ctx.enter_context(nc.psum_tensor(f"scores{b}", [P, BANK], F32)) for b in range(S_BANKS)]
        t_bank = [ctx.enter_context(nc.psum_tensor(f"turned{b}", [P, BANK], F32)) for b in range(T_BANKS)]
        j_bank = [ctx.enter_context(nc.psum_tensor(f"job{b}", [P, BANK], F32)) for b in range(J_BANKS)]
        o_bank = ctx.enter_context(nc.psum_tensor("mixed", [P, BANK], F32))

        big = sb("big", [P, max(2 * KT * SEQ, 2 * YT * D)], F16)
        hT = big[:, 0:2 * KT * SEQ].rearrange("p (h k s) -> p h k s", h=2, k=KT)
        wo = big[:, 0:2 * YT * D].rearrange("p (h k n) -> p h k n", h=2, k=YT)
        st_len = max(6 * SEQ, 5 * 2 * D)
        stack_flat = sb("stack", [P, st_len], F16)
        stack = stack_flat[:, 0:6 * SEQ].rearrange("p (a s) -> p a s", a=6)
        planes = sb("planes", [P, 4, max(SEQ, KT * MEM_LEN)], F16)
        values = [sb(f"values{b}", [P, NT, 2, P], F16) for b in range(2)]
        rows_flat = sb("rows", [P, ROWS * max(SEQ, 2048)], F32)
        rows = rows_flat[:, 0:ROWS * max(SEQ, 2048)].rearrange("p (r s) -> p r s", r=ROWS)
        ws = sb("ws", [P, 2, KT * P], F32)
        wt = sb("wt", [P, 4, 2, KT, P], F16)
        turned = sb("turned_halves", [P, PT_RING, 2, BANK], F16)
        temps = sb("temps", [P, max(5 * BANK, SEQ)], F32)
        e_buf = [temps[:, b * BANK:(b + 1) * BANK] for b in range(3)]
        c_buf = [temps[:, (3 + b) * BANK:(4 + b) * BANK] for b in range(2)]
        c_rows = temps[0:3, 0:SEQ].bitcast(BF16).rearrange("p (h s) -> p h s", h=2)
        ident = sb("ident", [P, P], F32)
        ident_b = sb("ident_b", [P, P], BF16)
        strict = sb("strict", [P, P], BF16)
        causal = sb("causal", [P, P], BF16)
        near_f = sb("near_f", [P, 2 * P], F32)
        near = sb("near", [P, 3, 2 * P], BF16)
        ones3 = sb("ones3", [3, P], BF16)
        neg_lam = sb("neg_lam", [P, 1], F32)
        head_gain = sb("head_gain", [P, P], F32)
        y_halves = sb("y_out_halves", [P, 2, 2, BANK], F16)
        gate_e = sb("gate_e", [P, P], F32)
        gate_f = sb("gate_f", [P, P], F32)
        gate_s = sb("gate_s", [P, P], F32)
        o_copy = sb("o_copy", [P, P], F32)
        junk = sb("junk", [P, P], F32)
        y_f = sb("y_f", [P, 2, P], F32)
        mx = sb("mx", [P, ROWS, 4], F32)
        neg_max = sb("neg_max", [P, ROWS], F32)
        z_sum = sb("z_sum", [P, ROWS], F32)
        rz = sb("rz", [P, 2], F32)
        sc = sb("sc", [P, 16], F32)
        gain = sb("gain", [P, 2, KT], F32)
        eps = sb("eps", [P, 1], F32)
        one = sb("one", [P, 1], F32)

        TILES = MEM_T + NT
        x_in = [rows[:, 0, 0:D], rows[:, 0, D:2 * D], rows[:, 1, 0:D]]
        x_n = [rows[:, 1, D:2 * D], rows[:, 2, 0:D]]
        x_g = [rows[:, 2, D:2 * D], rows[:, 3, 0:D]]
        tile_banks = [(s_bank[0], s_bank[1]), (t_bank[0], t_bank[1])]
        memT = planes[:, 0:2, 0:KT * MEM_LEN].rearrange("p h (k s) -> p h k s", k=KT)
        HALF = KT // 2
        km_sb = values[1][:, 0:4].rearrange("p a b c -> p (a b c)").rearrange("p (h s) -> p h s", h=2)
        vm_sb = values[0][:, 0:1].rearrange("p a b c -> p (a b) c")
        f_w = turned[:, 0].rearrange("p a b -> p (a b)")[:, 0:2 * KT * HEADS_FOX] \
            .rearrange("p (h k n) -> p h k n", h=2, k=KT)
        f_wf = junk[:, 0:KT * HEADS_FOX]
        pick_sb = stack_flat[0:BUCKETS, 0:2 * DIST_W].bitcast(F32)
        dmask_sb = stack_flat[0:UNITS, 2 * DIST_W:4 * DIST_W].bitcast(F32)
        rel_sb = stack_flat[0:BUCKETS, 4 * DIST_W:4 * DIST_W + 2 * UNITS].bitcast(F32)
        dist_sb = stack_flat[0:UNITS, 4 * DIST_W + 16:6 * DIST_W + 16].bitcast(F32)
        lam_sb = stack_flat[:, 6 * DIST_W + 16:6 * DIST_W + 16 + 8 * HEAD_DIM].bitcast(F32)
        b_sb = sc[0:HEADS_FOX, 15:16]
        fl = [rows[0:HEADS_FOX, r, 0:SEQ] for r in range(4)]
        c_parts = planes[0:HEADS_FOX, 0:3, 0:SEQ].bitcast(BF16)

        tile_in = [sem(f"tile_in{b}") for b in range(3)]
        consts_in, pool_made, consts_made = sem("consts_in"), sem("pool_made"), sem("consts_made")
        root_ready, norm_step, tile_n, tile_t, tile_g, tile_hi, tile_done = (
            sem(n) for n in ("root_ready", "norm_step", "tile_n", "tile_t", "tile_g", "tile_hi", "tile_done"))
        mw_in = [sem(f"mw_in{b}") for b in range(2)]
        mw_hi, mw_ready, mj_full, mj_hi, mj_done = (
            sem(n) for n in ("mw_hi", "mw_ready", "mj_full", "mj_hi", "mj_done"))
        m_stored = [sem(f"m_stored{b}") for b in range(2)]
        f_full, f_step, f_act, lam_step, lam_exp, lam_done, pre_stored, dist_full, dist_ready, near_stored = (
            sem(n) for n in ("f_full", "f_step", "f_act", "lam_step", "lam_exp", "lam_done", "pre_stored",
                             "dist_full", "dist_ready", "near_stored"))
        F_STEPS = NC + 8
        MEM_JOBS = [(s, t) for s in range(2 * UNITS) for t in ((0,) if s < UNITS else range(MEM_T))]

        def mem_count(s):
            return 1 if s < UNITS else MEM_T

        def mem_first(s):
            return sum(mem_count(r) for r in range(s))

        def km_view(n):
            return km_sb[:, :, (n % 2) * MEM_LEN:(n % 2 + 1) * MEM_LEN]

        def vm_view(n):
            return values[0][:, n % 4]

        def mem_out(n):
            s, t = MEM_JOBS[n]
            if s < UNITS:
                return j_bank[n % 2][:, 0:MEM_LEN], km_view(n)
            return j_bank[n % 2][:, 0:P], vm_view(n)

        def mem_high(act, n):
            act.wait_ge(mj_full, n + 1)
            if n >= 2:
                act.wait_ge(m_stored[n % 2], 16 * (n // 2))
            src, dst = mem_out(n)
            nc.scalar.activation(dst[:, 0], src, ACT.Copy, scale=1.0 / W_SCALE).then_inc(mj_hi, 1)

        def mem_low(dve, n):
            dve.wait_ge(mj_hi, n + 1)
            src, dst = mem_out(n)
            nc.vector.scalar_tensor_tensor(dst[:, 1], src, 1.0 / W_SCALE, dst[:, 0], op0=ALU.mult,
                                           op1=ALU.subtract).then_inc(mj_done, 1)

        def junk_lam(a):
            return y_f[:, a, 0:HEAD_DIM]

        with nc.Block() as block:
            @block.sync
            def _(sp):
                def load_tile(a):
                    src = mem[0, a * P:(a + 1) * P, :] if a < MEM_T else x[0, (a - MEM_T) * P:(a - MEM_T + 1) * P, :]
                    if a >= 3:
                        sp.wait_ge(tile_n, a - 2)
                    sp.dma_start(x_in[a % 3], src).then_inc(tile_in[a % 3], 16)

                for a in range(3):
                    load_tile(a)
                sp.dma_start(gain[:, 0, :], mem_norm[0].rearrange("(k p) -> p k", p=P), allow_slow_non_contiguous=True).then_inc(consts_in, 16)
                sp.dma_start(gain[:, 1, :], pre_norm[0].rearrange("(k p) -> p k", p=P), allow_slow_non_contiguous=True).then_inc(consts_in, 16)
                sp.dma_start(b_sb, b_forget[0].rearrange("(h a) -> h a", a=1)).then_inc(consts_in, 16)
                sp.dma_start(pick_sb, pick).then_inc(consts_in, 16)
                sp.dma_start(dmask_sb, dmask).then_inc(consts_in, 16)
                sp.dma_start(rel_sb, rel_bias).then_inc(consts_in, 16)
                sp.dma_start(lam_sb, diff_lambda[0].rearrange("a d -> (a d)").partition_broadcast(P)) \
                    .then_inc(consts_in, 16)
                sp.dma_start(head_gain[:, :], diff_head_norm[0].partition_broadcast(P)).then_inc(consts_in, 16)
                sp.dma_start(f_wf.rearrange("p (k n) -> p k n", k=KT),
                             w_cols[:, :, COL_FORGET:COL_FORGET + HEADS_FOX]).then_inc(consts_in, 16)
                for a in range(3, TILES):
                    load_tile(a)
                for s in range(2 * UNITS):
                    if s >= 2:
                        sp.wait_ge(mw_ready, s - 1)
                    sp.dma_start(ws[:, s % 2, :].rearrange("p (k n) -> p k n", k=KT),
                                 w_mem_cols[:, :, s * P:(s + 1) * P]).then_inc(mw_in[s % 2], 16)
                sp.wait_ge(dist_ready, 1)
                sp.dma_start(dist_dram, dist_sb).then_inc(near_stored, 16)
                sp.wait_ge(near_stored, 16)
                for h in range(UNITS):
                    sp.dma_start(near_dram[h], bass.AP(dist_dram.tensor, h * DIST_W, [[1, P], [1, 2 * P]])) \
                        .then_inc(pre_stored, 16)
                sp.wait_ge(f_step, F_STEPS)
                for part in range(3):
                    sp.dma_start(c_dram[part], c_parts[:, part, :]).then_inc(pre_stored, 16)
                for b in range(2):
                    sp.wait_ge(m_stored[b], 16 * len(MEM_JOBS) // 2)
                sp.wait_ge(pre_stored, 16 * (3 + UNITS))

            @block.gpsimd
            def _(pool):
                nc.gpsimd.memset(ident[:, :], 0.0).then_inc(pool_made, 1)
                nc.gpsimd.memset(o_copy[:, :], 0.0).then_inc(pool_made, 1)
                nc.gpsimd.memset(gate_e[:, :], 0.0).then_inc(pool_made, 1)
                pool.wait_ge(pool_made, 3)
                nc.gpsimd.affine_select(out=ident[:, :], in_=ident[:, :], compare_op=ALU.not_equal, fill=1.0,
                                        base=0, pattern=[[-1, P]], channel_multiplier=1).then_inc(pool_made, 1)
                nc.gpsimd.affine_select(out=o_copy[:, :], in_=o_copy[:, :], compare_op=ALU.is_gt, fill=NEG,
                                        base=0, pattern=[[-1, P]], channel_multiplier=1).then_inc(pool_made, 1)
                nc.gpsimd.affine_select(out=gate_e[:, :], in_=gate_e[:, :], compare_op=ALU.is_ge, fill=NEG,
                                        base=0, pattern=[[-1, P]], channel_multiplier=1).then_inc(pool_made, 1)
                for n, (s, t) in enumerate(MEM_JOBS):
                    pool.wait_ge(mj_done, n + 1)
                    if s < UNITS:
                        pool.dma_start(km_dram[s], km_view(n)).then_inc(m_stored[n % 2], 16)
                    else:
                        pool.dma_start(vm_dram[t, s - UNITS], vm_view(n)).then_inc(m_stored[n % 2], 16)

            @block.scalar
            def _(act):
                nc.scalar.preload_act_table_set("natural_log_exp_and_others")
                act.wait_ge(consts_made, 6)

                def root(a):
                    act.wait_ge(tile_in[a % 3], 16 * (a // 3 + 1))
                    if a >= 2:
                        act.wait_ge(tile_t, a - 1)
                    nc.scalar.activation(x_n[a % 2], x_in[a % 3], ACT.Square,
                                         accum_out=sc[:, a % 2:a % 2 + 1]).then_inc(norm_step, 1)
                    act.wait_ge(norm_step, 3 * a + 1)
                    nc.scalar.activation(sc[:, 2 + a % 2:3 + a % 2], sc[:, a % 2:a % 2 + 1], ACT.Ln,
                                         scale=1.0 / D, bias=eps[:, :]).then_inc(norm_step, 1)
                    act.wait_ge(norm_step, 3 * a + 2)
                    nc.scalar.activation(sc[:, 4 + a % 2:5 + a % 2], sc[:, 2 + a % 2:3 + a % 2], ACT.Exp,
                                         scale=-0.5).then_inc(norm_step, 1)

                def high(a):
                    act.wait_ge(tile_g, 2 * a + 2)
                    if a < MEM_T:
                        dst = memT[:, 0, :, a * P:(a + 1) * P]
                    else:
                        dst = hT[:, 0, :, (a - MEM_T) * P:(a - MEM_T + 1) * P]
                    nc.scalar.copy(dst, x_g[a % 2].rearrange("p (k s) -> p k s", k=KT)).then_inc(tile_hi, 1)

                for a in range(TILES):
                    root(a)
                    if a >= 1:
                        high(a - 1)
                high(TILES - 1)
                act.wait_ge(lam_step, 2)
                nc.scalar.activation(sc[:, 12:14], sc[:, 10:12], ACT.Exp).then_inc(lam_exp, 1)
                n = 0
                for s in range(2 * UNITS):
                    act.wait_ge(mw_in[s % 2], 16 * (s // 2 + 1))
                    if s >= 4:
                        act.wait_ge(mj_full, mem_first(s - 3))
                    nc.scalar.activation(wt[:, s % 4, 0], ws[:, s % 2, :].rearrange("p (k n) -> p k n", k=KT),
                                         ACT.Copy, scale=W_SCALE).then_inc(mw_hi, 1)
                    if s >= 1:
                        for _ in range(mem_count(s - 1)):
                            mem_high(act, n)
                            n += 1
                for _ in range(mem_count(2 * UNITS - 1)):
                    mem_high(act, n)
                    n += 1
                act.wait_ge(f_step, NC + 1)
                nc.scalar.activation(fl[1], fl[1], ACT.Exp, scale=-1.0).then_inc(f_act, 1)
                act.wait_ge(f_act, 1)
                nc.scalar.activation(fl[1], fl[1], ACT.Ln, bias=one[0:HEADS_FOX, :]).then_inc(f_act, 1)

            @block.vector
            def _(dve):
                nc.vector.memset(eps[:, :], EPS).then_inc(consts_made, 1)
                nc.vector.memset(one[:, :], 1.0).then_inc(consts_made, 1)
                nc.vector.memset(ones3[:, :], 1.0).then_inc(consts_made, 1)
                dve.wait_ge(pool_made, 6)
                nc.vector.tensor_copy(ident_b[:, :], ident[:, :]).then_inc(consts_made, 1)
                nc.vector.tensor_copy(strict[:, :], o_copy[:, :]).then_inc(consts_made, 1)
                nc.vector.tensor_copy(causal[:, :], gate_e[:, :]).then_inc(consts_made, 1)
                dve.wait_ge(consts_in, 16 * 9)
                nc.vector.tensor_scalar(head_gain[:, :], head_gain[:, :], 1.0 - LAM_INIT, None, ALU.mult) \
                    .then_inc(consts_made, 1)
                nc.vector.tensor_scalar(f_w[:, 0], f_wf.rearrange("p (k n) -> p k n", k=KT), W_SCALE, None,
                                        ALU.mult).then_inc(consts_made, 1)
                dve.wait_ge(consts_made, 8)
                nc.vector.scalar_tensor_tensor(f_w[:, 1], f_wf.rearrange("p (k n) -> p k n", k=KT), W_SCALE,
                                               f_w[:, 0], op0=ALU.mult, op1=ALU.subtract).then_inc(consts_made, 1)
                for a in range(2):
                    nc.vector.tensor_tensor_reduce(
                        out=junk_lam(a), in0=lam_sb[:, 2 * a * HEAD_DIM:(2 * a + 1) * HEAD_DIM],
                        in1=lam_sb[:, (2 * a + 1) * HEAD_DIM:(2 * a + 2) * HEAD_DIM], scale=1.0, scalar=0.0,
                        op0=ALU.mult, op1=ALU.add, accum_out=sc[:, 10 + a:11 + a]).then_inc(lam_step, 1)

                def norm(a):
                    s0, r0, v, h = (sc[:, c + a % 2:c + a % 2 + 1] for c in (0, 4, 6, 8))
                    dve.wait_ge(norm_step, 3 * a + 3)
                    nc.vector.tensor_scalar(v, s0, 1.0 / D, EPS, ALU.mult, ALU.add).then_inc(root_ready, 1)
                    dve.wait_ge(root_ready, 4 * a + 1)
                    nc.vector.tensor_scalar(v, v, r0, r0, ALU.mult, ALU.mult).then_inc(root_ready, 1)
                    dve.wait_ge(root_ready, 4 * a + 2)
                    nc.vector.tensor_scalar(v, v, -0.5, 1.5, ALU.mult, ALU.add).then_inc(root_ready, 1)
                    dve.wait_ge(root_ready, 4 * a + 3)
                    nc.vector.tensor_tensor(h, v, r0, ALU.mult).then_inc(root_ready, 1)
                    dve.wait_ge(root_ready, 4 * a + 4)
                    nc.vector.tensor_scalar(x_n[a % 2], x_in[a % 3], h, None, ALU.mult).then_inc(tile_n, 1)

                def gained(a):
                    dve.wait_ge(tile_t, a + 1)
                    for b in range(2):
                        g = gain[:, 0 if a < MEM_T else 1, b * HALF:(b + 1) * HALF]
                        nc.vector.tensor_tensor(
                            x_g[a % 2][:, b * HALF * P:(b + 1) * HALF * P].rearrange("p (k s) -> p k s", k=HALF),
                            tile_banks[a % 2][b][:, :].rearrange("p (k s) -> p k s", k=HALF),
                            g.unsqueeze(2).to_broadcast([P, HALF, P]), ALU.mult).then_inc(tile_g, 1)
                    dve.wait_ge(tile_hi, a + 1)
                    if a < MEM_T:
                        dst = memT[:, :, :, a * P:(a + 1) * P]
                    else:
                        dst = hT[:, :, :, (a - MEM_T) * P:(a - MEM_T + 1) * P]
                    nc.vector.tensor_tensor(dst[:, 1], x_g[a % 2].rearrange("p (k s) -> p k s", k=KT), dst[:, 0],
                                            ALU.subtract).then_inc(tile_done, 1)

                for a in range(TILES):
                    norm(a)
                    if a >= 1:
                        gained(a - 1)
                gained(TILES - 1)
                dve.wait_ge(lam_exp, 1)
                nc.vector.tensor_tensor(sc[:, 14:15], sc[:, 13:14], sc[:, 12:13], ALU.subtract).then_inc(lam_done, 1)
                dve.wait_ge(lam_done, 1)
                nc.vector.tensor_scalar(neg_lam[:, :], sc[:, 14:15], -LAM_INIT, None, ALU.add).then_inc(lam_done, 1)
                dve.wait_ge(dist_full, 1)
                nc.vector.tensor_tensor(dist_sb, t_bank[0][0:UNITS, 0:DIST_W], dmask_sb, ALU.add) \
                    .then_inc(dist_ready, 1)
                n = 0
                for s in range(2 * UNITS):
                    dve.wait_ge(mw_hi, s + 1)
                    nc.vector.scalar_tensor_tensor(
                        wt[:, s % 4, 1], ws[:, s % 2, :].rearrange("p (k n) -> p k n", k=KT), W_SCALE,
                        wt[:, s % 4, 0], op0=ALU.mult, op1=ALU.subtract).then_inc(mw_ready, 1)
                    if s >= 1:
                        for _ in range(mem_count(s - 1)):
                            mem_low(dve, n)
                            n += 1
                for _ in range(mem_count(2 * UNITS - 1)):
                    mem_low(dve, n)
                    n += 1
                for c in range(NC):
                    dve.wait_ge(f_full, c + 1)
                    nc.vector.tensor_scalar(fl[0][:, c * BANK:(c + 1) * BANK], s_bank[c % 2][0:HEADS_FOX, :],
                                            1.0 / W_SCALE, b_sb, ALU.mult, ALU.add).then_inc(f_step, 1)
                dve.wait_ge(f_step, NC)
                nc.vector.scalar_tensor_tensor(fl[1], fl[0], -1.0, fl[0], op0=ALU.mult, op1=ALU.max).then_inc(f_step, 1)
                dve.wait_ge(f_act, 2)
                nc.vector.scalar_tensor_tensor(fl[1], fl[0], 0.0, fl[1], op0=ALU.min,
                                               op1=ALU.subtract).then_inc(f_step, 1)
                dve.wait_ge(f_step, NC + 2)
                nc.vector.tensor_tensor_scan(out=fl[2], data0=fl[1], data1=fl[1], initial=0.0, op0=ALU.add,
                                             op1=ALU.bypass).then_inc(f_step, 1)
                dve.wait_ge(f_step, NC + 3)
                nc.vector.tensor_scalar(c_parts[:, 0], fl[2], -1.0, None, ALU.mult).then_inc(f_step, 1)
                dve.wait_ge(f_step, NC + 4)
                nc.vector.scalar_tensor_tensor(fl[3], fl[2], -1.0, c_parts[:, 0], op0=ALU.mult,
                                               op1=ALU.subtract).then_inc(f_step, 1)
                dve.wait_ge(f_step, NC + 5)
                nc.vector.tensor_copy(c_parts[:, 1], fl[3]).then_inc(f_step, 1)
                dve.wait_ge(f_step, NC + 6)
                nc.vector.tensor_tensor(fl[3], fl[3], c_parts[:, 1], ALU.subtract).then_inc(f_step, 1)
                dve.wait_ge(f_step, NC + 7)
                nc.vector.tensor_copy(c_parts[:, 2], fl[3]).then_inc(f_step, 1)

            @block.tensor
            def _(pe):
                pe.wait_ge(pool_made, 6)
                for a in range(TILES):
                    pe.wait_ge(tile_n, a + 1)
                    if a >= 2:
                        pe.wait_ge(tile_g, 2 * a - 2)
                    for k in range(KT):
                        last = nc.tensor.transpose(
                            tile_banks[a % 2][k // HALF][:, (k % HALF) * P:(k % HALF + 1) * P],
                            x_n[a % 2][:, k * P:(k + 1) * P], ident[:, :])
                    last.then_inc(tile_t, 1)
                pe.wait_ge(consts_in, 16 * 9)
                pe.wait_ge(tile_g, 2 * TILES)
                nc.tensor.matmul(t_bank[0][0:UNITS, 0:DIST_W], rel_sb, pick_sb, start=True, stop=True) \
                    .then_inc(dist_full, 1)
                pe.wait_ge(tile_done, TILES)
                for n, (s, t) in enumerate(MEM_JOBS):
                    pe.wait_ge(mw_ready, s + 1)
                    if n >= 2:
                        pe.wait_ge(mj_done, n - 1)
                    dst, _ = mem_out(n)
                    w = wt[:, s % 4]
                    for k in range(KT):
                        for a, b in ((0, 0), (0, 1), (1, 0)):
                            if s < UNITS:
                                lhs, rhs = w[:, a, k, :], memT[:, b, k, :]
                            else:
                                lhs, rhs = memT[:, a, k, t * P:(t + 1) * P], w[:, b, k, :]
                            last = nc.tensor.matmul(dst, lhs, rhs, start=(k == 0 and a == b == 0),
                                                    stop=(k == KT - 1 and a == 1))
                    last.then_inc(mj_full, 1)
                for c in range(NC):
                    if c >= 2:
                        pe.wait_ge(f_step, c - 1)
                    for k in range(KT):
                        for a, b in ((0, 0), (0, 1), (1, 0)):
                            last = nc.tensor.matmul(
                                s_bank[c % 2][0:HEADS_FOX, :], f_w[:, a, k, :],
                                hT[:, b, k, c * BANK:(c + 1) * BANK], start=(k == 0 and a == b == 0),
                                stop=(k == KT - 1 and a == 1))
                    last.then_inc(f_full, 1)

        s_full, s_free, stick_e, stick_abs, stick_ln, stick_sp, stick_sum = (
            sem(n) for n in ("s_full", "s_free", "stick_e", "stick_abs", "stick_ln", "stick_sp", "stick_sum"))
        max_ready, coef_step, combined, probs_ready = (
            sem(n) for n in ("max_ready", "coef_step", "combined", "probs_ready"))
        t_full, t_hi, t_free, pv_done, o_copied = (
            sem(n) for n in ("t_full", "t_hi", "t_free", "pv_done", "o_copied"))
        j_full, j_hi, j_free = (sem(n) for n in ("j_full", "j_hi", "j_free"))
        gate_exp, gate_done, gate_ln, var_ready, var_ln, root_done, post_step = (
            sem(n) for n in ("gate_exp", "gate_done", "gate_ln", "var_ready", "var_ln", "root_done", "post_step"))
        y_stored = [sem(f"y_stored{b}") for b in range(2)]
        w_in_sem = [sem(f"w_landed{b}") for b in range(2)]
        w_hi, w_ready = sem("w_hi"), sem("w_ready")
        stacked = [sem(f"stacked{c}") for c in range(NC)]
        c_landed, near_landed, near_step, mem_landed = (
            sem(n) for n in ("c_landed", "near_landed", "near_step", "mem_landed"))
        loop_sems = [s_full, s_free, stick_e, stick_abs, stick_ln, stick_sp, stick_sum, max_ready,
                     coef_step, combined, probs_ready, t_full, t_hi, t_free, pv_done, o_copied, j_full, j_hi, j_free, gate_exp,
                     gate_done, gate_ln, var_ready, var_ln, root_done, post_step, *y_stored, *w_in_sem, w_hi,
                     w_ready, *stacked, c_landed, near_landed, near_step, mem_landed]

        N_G = plan.n_steps
        KINDS = [UNIT[t].kind for t, _ in plan.steps]
        SOFT = [g for g in range(N_G) if KINDS[g] != "stick"]
        ROW_OF = {}
        for g in SOFT:
            for m in range(2 if KINDS[g] in ("forget", "diff") else 1):
                ROW_OF[g, m] = len(ROW_OF)
        DIFF_STEP = {g: n for n, g in enumerate([g for g in range(N_G) if KINDS[g] == "diff"])}
        DIFF_TAU = min(tau for g in DIFF_STEP for tau, _, _, _ in plan.t_chunks[g])
        STACKED = [16 + 64 * t for t in range(len(UNIT))]
        COEF = 3
        POST = {"stick": 1, "forget": 2, "mem": 2, "diff": 9}
        POST_AT, total = {}, 0
        for g in range(N_G):
            POST_AT[g] = total
            total += POST[KINDS[g]]
        Y_GROUPS = N_G // 4
        STORE = 16
        STICK = next(t for t, u in enumerate(UNIT) if u.kind == "stick")
        last_conv = {}
        for p in range(N_G):
            t, i = plan.steps[p]
            done = [plan.conv_of[t, G]] + [plan.conv_of[t + 1, kind] for kind in (V, Q, K)[:min(i, 2) + 1]
                                           if t + 1 < len(UNIT)]
            last_conv[p] = max(done)
        KM = values[1][:, 2:4].rearrange("p a b c -> p (a b c)").rearrange("p (h s) -> p h s", h=2)

        def row(g, m):
            return rows[:, (2 * g + m) % ROWS, :]

        def col(g, m):
            return slice((2 * g + m) % ROWS, (2 * g + m) % ROWS + 1)

        def mixed(g):
            return plan.t_chunks[g][-1][0] + 1

        def last_group_job(t, c):
            return plan.qk_jobs[t, c]

        def job_out(j):
            n, what, t, kind, index = j
            bank = j_bank[n % J_BANKS]
            if what == "qk":
                scale = (UNIT[t].scale if kind == Q else 1.0) / W_SCALE
                hi, lo = (HQ, LQ) if kind == Q else (HK, LK)
                at = slice(index * BANK, (index + 1) * BANK)
                return bank[:, :], planes[:, hi, at], planes[:, lo, at], scale
            if what == "v":
                v = values[UNIT[t].slot][:, index]
                return bank[:, 0:P], v[:, 0], v[:, 1], 1.0 / W_SCALE
            if what == "g":
                return bank[:, 0:P], None, None, 1.0 / W_SCALE
            at = slice(index % 4 * P, (index % 4 + 1) * P)
            y = y_halves[:, index // 4 % 2]
            return bank[:, 0:P], y[:, 0, at], y[:, 1, at], 1.0

        with nc.Fori(0, UNITS) as it:
            with nc.Block() as block:
                @block.sync
                def _(sp):
                    def load_weights(c):
                        n, t, kind = c
                        if n >= 2:
                            sp.wait_ge(w_ready, n - 1)
                        sp.dma_start(ws[:, n % 2, :].rearrange("p (k n) -> p k n", k=KT),
                                     w_cols[:, :, bass.ds(UNIT[t].col[kind] + it * P, P)]) \
                            .then_inc(w_in_sem[n % 2], 16)

                    every = [op[1] for op in plan.script if op[0] == "convert"]
                    issued = 0

                    def load_up_to(n):
                        nonlocal issued
                        while issued < min(n, len(every)):
                            load_weights(every[issued])
                            issued += 1

                    load_up_to(2)
                    sp.dma_start(values[1][:, 0:MEM_T].rearrange("p a b c -> p a (b c)"),
                                 vm_dram[:, bass.ds(it, 1)].rearrange("t u p h n -> p (u t) (h n)")) \
                        .then_inc(mem_landed, 16)
                    sp.dma_start(KM, km_dram[bass.ds(it, 1)].rearrange("u p h s -> p (u h) s")) \
                        .then_inc(mem_landed, 16)
                    sp.dma_start(near_f[:, :], near_dram[bass.ds(it, 1)].rearrange("a p n -> (a p) n")) \
                        .then_inc(near_landed, 16)
                    for p in range(N_G + 2):
                        if p < N_G:
                            t, i = plan.steps[p]
                            if i == 0:
                                if t:
                                    sp.wait_ge(s_full, plan.last_chunk[t - 1])
                                for c in range(NC):
                                    sp.wait_ge(j_free, last_group_job(t, c) + 1)
                                    at = slice(c * BANK, (c + 1) * BANK)
                                    if not UNIT[t].has_k:
                                        sp.dma_start(stack[:, 0:2, at], planes[:, HQ:LQ + 1, at]) \
                                            .then_inc(stacked[c], 16)
                                        continue
                                    for h in range(2):
                                        src = planes[h * 64:h * 64 + 64, :, at]
                                        dst = stack[:, 3 * h:3 * h + 3, at]
                                        sp.dma_start(dst[0:64], src[:, 0:3, :]).then_inc(stacked[c], 16)
                                        sp.dma_start(dst[64:128], src[:, 3:0:-1, :]).then_inc(stacked[c], 16)
                            if i == 0 and KINDS[p] == "forget":
                                sp.wait_ge(s_free, plan.last_chunk[t - 1])
                                sp.dma_start(c_rows, c_dram[:, bass.ds(2 * it, 2), :]).then_inc(c_landed, 16)
                            load_up_to(sum(n <= last_conv[p] for n in range(len(every))) + 2)
                        g = p - 2
                        if g >= 0 and g % 4 == 3:
                            yg = g // 4
                            t, i = plan.steps[g]
                            sp.wait_ge(j_free, plan.y_job[g][0] + 1)
                            dst = y_dram.rearrange("h (u f) s -> u f h s", f=P)
                            sp.dma_start(dst[bass.ds(UNIT[t].group * UNITS + it, 1), :, :,
                                             (i - 3) * P:(i + 1) * P].rearrange("u f h s -> (u f) h s"),
                                         y_halves[:, yg % 2]).then_inc(y_stored[yg % 2], STORE)
                    for b in range(2):
                        sp.wait_ge(y_stored[b], STORE * Y_GROUPS // 2)

                @block.tensor
                def _(pe):
                    def bank_of(j):
                        n = j[0]
                        if n >= J_BANKS:
                            pe.wait_ge(j_free, n - J_BANKS + 1)
                        return j_bank[n % J_BANKS]

                    def part(j, k0, k1):
                        n, what, t, kind, index = j
                        if k0 == 0:
                            unit = plan.steps[index][0] if what == "g" else t
                            if index == (unit * NT if what == "g" else 0):
                                pe.wait_ge(w_ready, plan.conv_of[unit, kind] + 1)
                            bank_of(j)
                        bank = j_bank[n % J_BANKS]
                        if what == "qk":
                            dst = bank[:, :]
                            pairs = [(wt[:, kind, a, k, :], hT[:, b, k, index * BANK:(index + 1) * BANK])
                                     for k in range(k0, k1) for a, b in ((0, 0), (0, 1), (1, 0))]
                        else:
                            i = index if what == "v" else plan.steps[index][1]
                            dst = bank[:, 0:P]
                            pairs = [(hT[:, a, k, i * P:(i + 1) * P], wt[:, kind, b, k, :])
                                     for k in range(k0, k1) for a, b in ((0, 0), (0, 1), (1, 0))]
                        for q, (lhs, rhs) in enumerate(pairs):
                            last = nc.tensor.matmul(dst, lhs, rhs, start=(k0 == 0 and q == 0),
                                                    stop=(k1 == KT and q == len(pairs) - 1))
                        if k1 == KT:
                            last.then_inc(j_full, 1)

                    def scores(g, n, m, c, w):
                        t, i = plan.steps[g]
                        kind = KINDS[g]
                        if n == plan.chunks[g][0][0]:
                            if i % 4 == 0:
                                pe.wait_ge(stacked[i // 4], STACKED[t])
                            if kind == "forget" and i == 0:
                                pe.wait_ge(c_landed, 16)
                            if kind == "diff" and i == 0:
                                pe.wait_ge(near_step, 5)
                            if kind == "mem" and i == 0:
                                pe.wait_ge(mem_landed, 32)
                        if n >= S_BANKS:
                            pe.wait_ge(s_free, n - S_BANKS + 1)
                        bank = s_bank[n % S_BANKS]
                        parts = []
                        if kind == "mem":
                            for a, b in ((0, 0), (0, 1), (1, 0)):
                                parts.append((0, w, stack[:, a, i * P:(i + 1) * P], KM[:, b, :]))
                        else:
                            for a in (1, 2):
                                parts.append((0, w, stack[:, 3 * m + a, i * P:(i + 1) * P],
                                              stack[:, 3 * m, c:c + w]))
                        if kind == "forget":
                            parts.append((0, w, ones3[:, :], c_rows[:, m, c:c + w]))
                        if kind in ("stick", "forget") and c + w == (i + 1) * P:
                            parts.append((w - P, P, ident_b[:, :],
                                          (strict if kind == "stick" else causal)[:, :]))
                        if kind == "diff":
                            first = max(c, (i - 1) * P)
                            if first < c + w:
                                at, width = first - c, c + w - first
                                off = first - (i - 1) * P
                                for a in range(3):
                                    parts.append((at, width, ident_b[:, :], near[:, a, off:off + width]))
                        for q, (at, width, lhs, rhs) in enumerate(parts):
                            last = nc.tensor.matmul(bank[:, at:at + width], lhs, rhs, start=(q == 0),
                                                    stop=(q == len(parts) - 1), skip_group_check=True)
                        last.then_inc(s_full, 1)

                    def turn(g, tau, m, k0, tiles):
                        if KINDS[g] == "diff":
                            pe.wait_ge(combined, tau - DIFF_TAU + 1)
                        elif k0 == 0:
                            pe.wait_ge(probs_ready, plan.row_index[g, m] + 1)
                        if tau >= T_BANKS:
                            pe.wait_ge(t_free, tau - T_BANKS + 1)
                        for k in range(tiles):
                            last = nc.tensor.transpose(t_bank[tau % T_BANKS][:, k * P:(k + 1) * P],
                                                       row(g, m)[:, (k0 + k) * P:(k0 + k + 1) * P], ident[:, :])
                        last.then_inc(t_full, 1)

                    def mix(g, tau, m, k0, tiles, first, end):
                        unit = UNIT[plan.steps[g][0]]
                        if first and g:
                            pe.wait_ge(o_copied, g)
                        pe.wait_ge(t_free, tau + 1)
                        wide = P if KINDS[g] in ("diff", "mem") else HEAD_DIM
                        v = values[unit.slot]
                        for k in range(tiles):
                            for q, (a, b) in enumerate(((0, 0), (0, 1), (1, 0))):
                                last = nc.tensor.matmul(
                                    o_bank[:, m * HEAD_DIM:m * HEAD_DIM + wide],
                                    turned[:, tau % PT_RING, a, k * P:(k + 1) * P],
                                    v[:, k0 + k, b, m * HEAD_DIM:m * HEAD_DIM + wide],
                                    start=(first and k == 0 and q == 0), stop=(end and k == tiles - 1 and q == 2),
                                    skip_group_check=True)
                        last.then_inc(pv_done, 1)

                    for op, *args in plan.script:
                        if op == "part":
                            part(*args)
                        if op == "scores":
                            scores(args[0], *args[1])
                        if op == "turn":
                            turn(args[0], *args[1])
                        if op == "mix":
                            mix(args[0], *args[1], first=args[2], end=args[3])
                        if op == "y":
                            g = args[0]
                            bank = bank_of(plan.y_job[g])
                            pe.wait_ge(post_step, POST_AT[g] + POST[KINDS[g]])
                            nc.tensor.transpose(bank[:, 0:P], y_f[:, g % 2, :], ident[:, :]).then_inc(j_full, 1)

                @block.scalar
                def _(act):
                    def convert(c):
                        n, t, kind = c
                        act.wait_ge(w_in_sem[n % 2], (n // 2 + 1) * 16)
                        nc.scalar.activation(wt[:, kind, 0],
                                             ws[:, n % 2, :].rearrange("p (k n) -> p k n", k=KT), ACT.Copy,
                                             scale=W_SCALE).then_inc(w_hi, 1)

                    def high(j):
                        n, what, t, kind, index = j
                        src, dst, _, scale = job_out(j)
                        act.wait_ge(j_full, n + 1)
                        if what == "qk" and t:
                            act.wait_ge(stacked[index], STACKED[t - 1])
                        if what == "y" and index % 4 == 0:
                            yg = index // 4
                            act.wait_ge(y_stored[yg % 2], yg // 2 * STORE)
                        nc.scalar.activation(dst, src, ACT.Copy, scale=scale).then_inc(j_hi, 1)

                    def stick_exp(n, w):
                        e = e_buf[n % 3][:, 0:w]
                        act.wait_ge(s_full, n + 1)
                        at = n - plan.first_chunk[STICK]
                        nc.scalar.activation(e, s_bank[n % S_BANKS][:, 0:w], ACT.Abs).then_inc(stick_abs, 1)
                        act.wait_ge(stick_abs, at + 1)
                        nc.scalar.activation(e, e, ACT.Exp, scale=-1.0).then_inc(stick_e, 1)

                    def stick_log(n, w):
                        e = e_buf[n % 3][:, 0:w]
                        act.wait_ge(stick_e, n - plan.first_chunk[STICK] + 1)
                        nc.scalar.activation(e, e, ACT.Ln, bias=one[:, :]).then_inc(stick_ln, 1)

                    for op, *args in plan.script:
                        g = args[0]
                        if op == "convert":
                            convert(*args)
                        if op == "halves":
                            high(*args)
                        if op == "y":
                            high(plan.y_job[g])
                        if op == "scores" and KINDS[g] == "stick":
                            stick_exp(args[1][0], args[1][3])
                        if op == "log":
                            stick_log(args[1][0], args[1][3])
                        if op == "gate":
                            act.wait_ge(j_free, plan.gate_job[g][0] + 1)
                            nc.scalar.activation(gate_e[:, :], gate_f[:, :], ACT.Exp, scale=-1.0) \
                                .then_inc(j_hi, 1)
                        if op == "silu":
                            act.wait_ge(j_hi, plan.gate_job[g][0] + 1)
                            nc.scalar.activation(gate_e[:, :], gate_e[:, :], ACT.Ln, bias=one[:, :]) \
                                .then_inc(gate_ln, 1)
                            act.wait_ge(gate_ln, g + 1)
                            nc.scalar.activation(gate_e[:, :], gate_e[:, :], ACT.Exp, scale=-1.0) \
                                .then_inc(gate_exp, 1)
                        if op == "turn":
                            tau, m, k0, tiles = args[1]
                            w = tiles * P
                            act.wait_ge(t_full, tau + 1)
                            if tau >= PT_RING:
                                act.wait_ge(pv_done, tau - PT_RING + 1)
                            nc.scalar.copy(turned[:, tau % PT_RING, 0, 0:w], t_bank[tau % T_BANKS][:, 0:w]) \
                                .then_inc(t_hi, 1)
                        if op == "take":
                            act.wait_ge(pv_done, mixed(g))
                            if g:
                                act.wait_ge(post_step, POST_AT[g])
                            nc.scalar.copy(o_copy[:, :], o_bank[:, 0:P]).then_inc(o_copied, 1)
                        if op == "root":
                            d = DIFF_STEP[g]
                            act.wait_ge(var_ready, d + 1)
                            nc.scalar.activation(sc[:, 3:4], sc[:, 2:3], ACT.Ln).then_inc(var_ln, 1)
                            act.wait_ge(var_ln, d + 1)
                            nc.scalar.activation(sc[:, 4:5], sc[:, 3:4], ACT.Exp, scale=-0.5) \
                                .then_inc(root_done, 1)
                        if op == "probs":
                            m = args[1]
                            keys = 2 * P if KINDS[g] == "mem" else (plan.steps[g][1] + 1) * P
                            mine = row(g, m)[:, 0:keys]
                            if KINDS[g] == "stick":
                                n = max(ch[0] for ch in plan.chunks[g] if ch[1] == m)
                                act.wait_ge(s_free, n + 1)
                                nc.scalar.activation(mine, mine, ACT.Exp).then_inc(probs_ready, 1)
                            else:
                                act.wait_ge(max_ready, ROW_OF[g, m] + 1)
                                nc.scalar.activation(mine, mine, ACT.Exp, bias=neg_max[:, col(g, m)],
                                                     accum_out=z_sum[:, col(g, m)]).then_inc(probs_ready, 1)

                @block.vector
                def _(dve):
                    def low(j):
                        n, what, t, kind, index = j
                        src, hi, lo, scale = job_out(j)
                        dve.wait_ge(j_hi, n + 1)
                        nc.vector.scalar_tensor_tensor(lo, src, scale, hi, op0=ALU.mult, op1=ALU.subtract) \
                            .then_inc(j_free, 1)

                    def convert(c):
                        n, t, kind = c
                        dve.wait_ge(w_hi, n + 1)
                        nc.vector.scalar_tensor_tensor(
                            wt[:, kind, 1], ws[:, n % 2, :].rearrange("p (k n) -> p k n", k=KT), W_SCALE,
                            wt[:, kind, 0], op0=ALU.mult, op1=ALU.subtract).then_inc(w_ready, 1)

                    def stick_chunk(g, n, m, c, w):
                        at = n - plan.first_chunk[STICK]
                        e, s, z = e_buf[n % 3][:, 0:w], c_buf[n % 2][:, 0:w], s_bank[n % S_BANKS][:, 0:w]
                        dve.wait_ge(stick_ln, at + 1)
                        nc.vector.scalar_tensor_tensor(e, z, 0.0, e, op0=ALU.max, op1=ALU.add) \
                            .then_inc(stick_sp, 1)
                        dve.wait_ge(stick_sp, at + 1)
                        first = c + w == (plan.steps[g][1] + 1) * P
                        if not first:
                            dve.wait_ge(stick_sum, at)
                        start = 0.0 if first else c_buf[(n - 1) % 2][:, 0:1]
                        nc.vector.tensor_tensor_scan(out=s[:, ::-1], data0=e[:, ::-1], data1=e[:, ::-1],
                                                     initial=start, op0=ALU.add, op1=ALU.bypass) \
                            .then_inc(stick_sum, 1)
                        dve.wait_ge(stick_sum, at + 1)
                        nc.vector.tensor_tensor(row(g, m)[:, c:c + w], z, s, ALU.subtract).then_inc(s_free, 1)

                    def soft_chunk(g, n, m, c, w):
                        r = (2 * g + m) % ROWS
                        dve.wait_ge(s_full, n + 1)
                        nc.vector.tensor_scalar(row(g, m)[:, c:c + w], s_bank[n % S_BANKS][:, 0:w], 1.0,
                                                -3.0e38, ALU.mult, ALU.max,
                                                accum_out=mx[:, r, c // BANK:c // BANK + 1]).then_inc(s_free, 1)

                    def row_max(g, m):
                        mine = [ch for ch in plan.chunks[g] if ch[1] == m]
                        r = (2 * g + m) % ROWS
                        dve.wait_ge(s_free, mine[-1][0] + 1)
                        nc.vector.tensor_reduce(neg_max[:, r:r + 1], mx[:, r, 0:len(mine)], AX_X, ALU.max,
                                                negate=True).then_inc(max_ready, 1)

                    def combine(g, tau, m, k0, tiles):
                        at = DIFF_STEP[g] * COEF
                        if k0 == 0:
                            z0, z1 = z_sum[:, col(g, 0)], z_sum[:, col(g, 1)]
                            dve.wait_ge(probs_ready, plan.row_index[g, 1] + 1)
                            nc.vector.reciprocal(sc[:, 0:1], z1).then_inc(coef_step, 1)
                            dve.wait_ge(coef_step, at + 1)
                            nc.vector.tensor_tensor(sc[:, 0:1], sc[:, 0:1], z0, ALU.mult).then_inc(coef_step, 1)
                            dve.wait_ge(coef_step, at + 2)
                            nc.vector.tensor_tensor(sc[:, 1:2], sc[:, 0:1], neg_lam[:, :], ALU.mult) \
                                .then_inc(coef_step, 1)
                            dve.wait_ge(coef_step, at + 3)
                        s = slice(k0 * P, (k0 + tiles) * P)
                        nc.vector.scalar_tensor_tensor(row(g, 0)[:, s], row(g, 1)[:, s], sc[:, 1:2],
                                                       row(g, 0)[:, s], op0=ALU.mult, op1=ALU.add) \
                            .then_inc(combined, 1)

                    def take_gate(g):
                        dve.wait_ge(j_full, plan.gate_job[g][0] + 1)
                        if g:
                            dve.wait_ge(gate_done, g)
                        nc.vector.tensor_scalar(gate_f[:, :], job_out(plan.gate_job[g])[0], 1.0 / W_SCALE,
                                                GATE_MIN, ALU.mult, ALU.max).then_inc(j_free, 1)

                    def silu(g):
                        if g:
                            dve.wait_ge(post_step, POST_AT[g])
                        dve.wait_ge(gate_exp, g + 1)
                        nc.vector.tensor_tensor(gate_s[:, :], gate_f[:, :], gate_e[:, :], ALU.mult) \
                            .then_inc(gate_done, 1)

                    def variance(g):
                        at = POST_AT[g]
                        rz0 = rz[:, 0:1]
                        nc.vector.reciprocal(rz0, z_sum[:, col(g, 0)]).then_inc(post_step, 1)
                        dve.wait_ge(o_copied, g + 1)
                        nc.vector.tensor_tensor_reduce(out=junk[:, :], in0=o_copy[:, :], in1=o_copy[:, :],
                                                       scale=1.0, scalar=0.0, op0=ALU.mult, op1=ALU.add,
                                                       accum_out=sc[:, 6:7]).then_inc(post_step, 1)
                        dve.wait_ge(gate_done, g + 1)
                        nc.vector.tensor_tensor(gate_s[:, :], gate_s[:, :], head_gain[:, :], ALU.mult) \
                            .then_inc(post_step, 1)
                        dve.wait_ge(post_step, at + 3)
                        nc.vector.tensor_scalar(sc[:, 7:8], sc[:, 6:7], rz0, rz0, ALU.mult, ALU.mult) \
                            .then_inc(post_step, 1)
                        dve.wait_ge(post_step, at + 4)
                        nc.vector.tensor_scalar(sc[:, 2:3], sc[:, 7:8], 1.0 / P, EPS, ALU.mult, ALU.add) \
                            .then_inc(var_ready, 1)

                    def post(g):
                        kind = KINDS[g]
                        at = POST_AT[g]
                        y = y_f[:, g % 2, :]
                        if g >= 2:
                            dve.wait_ge(j_full, plan.y_job[g - 2][0] + 1)
                        dve.wait_ge(gate_done, g + 1)
                        if kind == "stick":
                            dve.wait_ge(o_copied, g + 1)
                            nc.vector.tensor_tensor(y, o_copy[:, :], gate_s[:, :], ALU.mult).then_inc(post_step, 1)
                        elif kind in ("forget", "mem"):
                            heads = 2 if kind == "forget" else 1
                            wide = P // heads
                            r = 2 * g % ROWS
                            nc.vector.reciprocal(rz[:, 0:heads], z_sum[:, r:r + heads]).then_inc(post_step, 1)
                            dve.wait_ge(post_step, at + 1)
                            dve.wait_ge(o_copied, g + 1)
                            for h in range(heads):
                                s = slice(h * wide, (h + 1) * wide)
                                last = nc.vector.scalar_tensor_tensor(y[:, s], o_copy[:, s], rz[:, h:h + 1],
                                                                      gate_s[:, s], op0=ALU.mult, op1=ALU.mult)
                            last.then_inc(post_step, 1)
                        else:
                            v, r0, h, rz0 = sc[:, 2:3], sc[:, 4:5], sc[:, 5:6], rz[:, 0:1]
                            dve.wait_ge(root_done, DIFF_STEP[g] + 1)
                            nc.vector.tensor_scalar(h, v, r0, r0, ALU.mult, ALU.mult).then_inc(post_step, 1)
                            dve.wait_ge(post_step, at + 5)
                            nc.vector.tensor_scalar(h, h, -0.5, 1.5, ALU.mult, ALU.add).then_inc(post_step, 1)
                            dve.wait_ge(post_step, at + 6)
                            nc.vector.tensor_tensor(h, h, r0, ALU.mult).then_inc(post_step, 1)
                            dve.wait_ge(post_step, at + 7)
                            nc.vector.tensor_tensor(h, h, rz0, ALU.mult).then_inc(post_step, 1)
                            dve.wait_ge(post_step, at + 8)
                            nc.vector.scalar_tensor_tensor(y, o_copy[:, :], h, gate_s[:, :], op0=ALU.mult,
                                                           op1=ALU.mult).then_inc(post_step, 1)

                    def split_near():
                        dve.wait_ge(near_landed, 16)
                        for a in range(3):
                            nc.vector.tensor_copy(near[:, a, :], near_f[:, ::-1]).then_inc(near_step, 1)
                            if a < 2:
                                dve.wait_ge(near_step, 2 * a + 1)
                                nc.vector.tensor_tensor(near_f[:, :], near_f[:, :], near[:, a, ::-1], ALU.subtract) \
                                    .then_inc(near_step, 1)
                                dve.wait_ge(near_step, 2 * a + 2)

                    for op, *args in plan.script:
                        g = args[0]
                        if op == "convert":
                            convert(*args)
                        if op == "halves":
                            low(*args)
                        if op == "y":
                            low(plan.y_job[g])
                        if op == "scores" and KINDS[g] != "stick":
                            if KINDS[g] == "diff" and args[1][0] == plan.first_chunk[plan.steps[g][0]]:
                                split_near()
                            soft_chunk(g, *args[1])
                        if op == "log":
                            stick_chunk(g, *args[1])
                        if op == "probs" and KINDS[g] != "stick":
                            row_max(g, args[1])
                        if op == "combine":
                            combine(g, *args[1])
                        if op == "turn":
                            tau, m, k0, tiles = args[1]
                            w = tiles * P
                            dve.wait_ge(t_hi, tau + 1)
                            nc.vector.tensor_tensor(turned[:, tau % PT_RING, 1, 0:w],
                                                    t_bank[tau % T_BANKS][:, 0:w],
                                                    turned[:, tau % PT_RING, 0, 0:w], ALU.subtract) \
                                .then_inc(t_free, 1)
                        if op == "gate":
                            take_gate(g)
                        if op == "silu":
                            silu(g)
                        if op == "variance":
                            variance(g)
                        if op == "post":
                            post(g)
            with nc.Block() as block:
                @block.gpsimd
                def _(pool):
                    for s in loop_sems:
                        nc.gpsimd.sem_clear(s)

        PAIRS = NT // 2
        yl = [rows_flat[:, b * YT * 2 * P:(b + 1) * YT * 2 * P].bitcast(F16)
              .rearrange("p (h k s) -> p h k s", h=2, k=YT) for b in range(2)]
        flat = stack_flat[:, 0:5 * 2 * D].bitcast(F32)
        x_res = [flat[:, b * D:(b + 1) * D] for b in range(2)]
        o_out = [flat[:, (2 + b) * D:(3 + b) * D] for b in range(2)]
        gain_out = flat[:, 4 * D:5 * D]
        out_banks = [(s_bank[0], s_bank[1]), (t_bank[0], t_bank[1])]
        scrap = [j_bank[0], j_bank[1]]
        wo_in, y_in, x_in2, out_stored = ([sem(f"{n}{b}") for b in range(2)]
                                          for n in ("wo_landed", "y_landed", "res_landed", "out_stored"))
        wo_hi, wo_ready, gain_in, out_full, out_sq, out_root, out_step, out_ready = (
            sem(n) for n in ("wo_hi", "wo_ready", "gain_landed", "out_full", "out_sq", "out_root", "out_step",
                             "out_ready"))
        var_sum = sem("var_sum")
        OUT_STEPS = 6
        with nc.Block() as block:
            @block.sync
            def _(sp):
                def load_y(q):
                    if q >= 2:
                        sp.wait_ge(out_full, 2 * (q - 1))
                    src = y_dram[:, :, q * 2 * P:(q + 1) * 2 * P].rearrange("h (k f) s -> f h k s", f=P)
                    for h in range(2):
                        sp.dma_start(yl[q % 2][:, h], src[:, h]).then_inc(y_in[q % 2], 16)

                for k in range(YT):
                    if k >= 2:
                        sp.wait_ge(wo_ready, k - 1)
                    sp.dma_start(ws[:, k % 2, :], w_out_rows[k]).then_inc(wo_in[k % 2], 16)
                    if k == 1:
                        load_y(0)
                        load_y(1)
                        sp.dma_start(gain_out, post_norm[0].partition_broadcast(P)).then_inc(gain_in, 16)
                for i in range(NT):
                    if i >= 2:
                        sp.wait_ge(out_ready, i - 1)
                    sp.dma_start(x_res[i % 2], x[0, i * P:(i + 1) * P, :]).then_inc(x_in2[i % 2], 16)
                    if i >= 1:
                        sp.wait_ge(out_ready, i)
                        sp.dma_start(out[0, (i - 1) * P:i * P, :], o_out[(i - 1) % 2]) \
                            .then_inc(out_stored[(i - 1) % 2], 16)
                    if i % 2 == 0 and i // 2 + 1 >= 2 and i // 2 + 1 < PAIRS:
                        load_y(i // 2 + 1)
                sp.wait_ge(out_ready, NT)
                sp.dma_start(out[0, (NT - 1) * P:NT * P, :], o_out[(NT - 1) % 2]) \
                    .then_inc(out_stored[(NT - 1) % 2], 16)
                for b in range(2):
                    sp.wait_ge(out_stored[b], 16 * (NT // 2))

            @block.tensor
            def _(pe):
                pe.wait_ge(wo_ready, YT)
                for i in range(NT):
                    if i % 2 == 0:
                        pe.wait_ge(y_in[i // 2 % 2], 32 * (i // 4 + 1))
                    if i >= 2:
                        pe.wait_ge(out_step, OUT_STEPS * (i - 1))
                    y = yl[i // 2 % 2]
                    for n in range(2):
                        for k in range(YT):
                            for a, b in ((0, 0), (0, 1), (1, 0)):
                                last = nc.tensor.matmul(
                                    out_banks[i % 2][n][:, :], y[:, a, k, (i % 2) * P:(i % 2 + 1) * P],
                                    wo[:, b, k, n * BANK:(n + 1) * BANK], start=(k == 0 and a == b == 0),
                                    stop=(k == YT - 1 and a == 1))
                    last.then_inc(out_full, 1)

            @block.scalar
            def _(act):
                for k in range(YT):
                    act.wait_ge(wo_in[k % 2], 16 * (k // 2 + 1))
                    nc.scalar.activation(wo[:, 0, k], ws[:, k % 2, :], ACT.Copy, scale=W_SCALE).then_inc(wo_hi, 1)
                for i in range(NT):
                    act.wait_ge(out_full, i + 1)
                    for n in range(2):
                        nc.scalar.activation(scrap[n][:, :], out_banks[i % 2][n][:, :], ACT.Square,
                                             scale=1.0 / W_SCALE, accum_out=sc[:, n:n + 1]).then_inc(out_sq, 1)
                    act.wait_ge(out_step, OUT_STEPS * i + 1)
                    nc.scalar.activation(sc[:, 3:4], sc[:, 2:3], ACT.Ln).then_inc(out_root, 1)
                    act.wait_ge(out_root, 2 * i + 1)
                    nc.scalar.activation(sc[:, 4:5], sc[:, 3:4], ACT.Exp, scale=-0.5).then_inc(out_root, 1)

            @block.vector
            def _(dve):
                for k in range(YT):
                    dve.wait_ge(wo_hi, k + 1)
                    nc.vector.scalar_tensor_tensor(wo[:, 1, k], ws[:, k % 2, :], W_SCALE, wo[:, 0, k],
                                                   op0=ALU.mult, op1=ALU.subtract).then_inc(wo_ready, 1)
                dve.wait_ge(gain_in, 16)
                for i in range(NT):
                    v, r0, h = sc[:, 2:3], sc[:, 4:5], sc[:, 5:6]
                    at = OUT_STEPS * i
                    dve.wait_ge(out_sq, 2 * i + 2)
                    nc.vector.tensor_tensor(sc[:, 6:7], sc[:, 0:1], sc[:, 1:2], ALU.add).then_inc(var_sum, 1)
                    dve.wait_ge(var_sum, i + 1)
                    nc.vector.tensor_scalar(v, sc[:, 6:7], 1.0 / D, EPS, ALU.mult, ALU.add).then_inc(out_step, 1)
                    dve.wait_ge(out_root, 2 * i + 2)
                    nc.vector.tensor_scalar(h, v, r0, r0, ALU.mult, ALU.mult).then_inc(out_step, 1)
                    dve.wait_ge(out_step, at + 2)
                    nc.vector.tensor_scalar(h, h, -0.5 / W_SCALE, 1.5 / W_SCALE, ALU.mult, ALU.add) \
                        .then_inc(out_step, 1)
                    dve.wait_ge(out_step, at + 3)
                    nc.vector.tensor_tensor(h, h, r0, ALU.mult).then_inc(out_step, 1)
                    dve.wait_ge(out_step, at + 4)
                    if i >= 2:
                        dve.wait_ge(out_stored[i % 2], 16 * (i // 2))
                    for n in range(2):
                        s = slice(n * BANK, (n + 1) * BANK)
                        nc.vector.scalar_tensor_tensor(o_out[i % 2][:, s], out_banks[i % 2][n][:, :], h,
                                                       gain_out[:, s], op0=ALU.mult, op1=ALU.mult) \
                            .then_inc(out_step, 1)
                    dve.wait_ge(out_step, at + 6)
                    dve.wait_ge(x_in2[i % 2], 16 * (i // 2 + 1))
                    nc.vector.tensor_tensor(o_out[i % 2], o_out[i % 2], x_res[i % 2], ALU.add) \
                        .then_inc(out_ready, 1)


NAMES = ["x", "mem", "w_in", "b_forget", "w_mem_kv", "w_out", "pre_norm", "post_norm", "mem_norm",
         "diff_lambda", "diff_head_norm", "rel_bias"]


def kernel(**inputs):
    import concourse.bacc as bacc
    from concourse.bass_utils import run_bass_kernel_spmd

    nc = bacc.Bacc("TRN2", target_bir_lowering=False, num_devices=1)
    arrays = {name: np.ascontiguousarray(inputs[name]) for name in NAMES}
    arrays["pick"], arrays["dmask"] = distance_tables(3 * P)
    args = [nc.dram_tensor(name, a.shape, mybir.dt.from_np(a.dtype), kind="ExternalInput").ap()
            for name, a in arrays.items()]
    shape = arrays["x"].shape
    args.append(nc.dram_tensor("out", shape, F32, kind="ExternalOutput").ap())
    build(nc, *args)
    result = run_bass_kernel_spmd(nc, [arrays], core_ids=[0])
    return result.results[0]["out"]
```

```python
from contextlib import ExitStack

import concourse.bass as bass
import numpy as np
from concourse import mybir

ALU = mybir.AluOpType
ACT = mybir.ActivationFunctionType
AX_X = mybir.AxisListType.X
F32 = mybir.dt.float32
F16 = mybir.dt.float16
BF16 = mybir.dt.bfloat16

P = 128
HEAD_DIM = 64
GROUP_W = 512
PAIR_W = 128
UNITS = GROUP_W // PAIR_W
BUCKETS = 32
MAX_DISTANCE = 128
EPS = 1e-6
NEG = -1e30
LAM_INIT = 0.2
W_SCALE = 64.0
GATE_MIN = -41.0
BANK = 512
MIX_LAG = 2
HOP = 0.15
STALL_W = 1.08
PACE = 0.017
BIAS = {"end": -0.51, "value": -0.02, "probs": 0.21, "score": 0.48, "gate": 0.0, "project": 0.92}
EARLY_V = {1: 16, 2: 8, 3: 12}
S_BANKS, T_BANKS, J_BANKS, PT_RING, ROWS = 3, 2, 2, 4, 4
Q, K, V, G = range(4)
HK, HQ, LQ, LK = range(4)

COL_FORGET = 9 * GROUP_W
HEADS_FOX = GROUP_W // HEAD_DIM
COL_MEM = COL_FORGET + HEADS_FOX
COL_GATE = COL_MEM + GROUP_W


class Unit:

    def __init__(self, kind, group, slot, scale):
        self.kind, self.group, self.slot, self.scale = kind, group, slot, scale
        base = 3 * GROUP_W * group
        self.col = {Q: base, K: base + GROUP_W, V: base + 2 * GROUP_W, G: COL_GATE + GROUP_W * group}
        if kind == "mem":
            self.col[Q] = COL_MEM
        self.has_k = kind != "mem"


UNIT = [
    Unit("mem", 3, 1, float(PAIR_W) ** -0.5),
    Unit("stick", 1, 0, HEAD_DIM ** -0.5),
    Unit("diff", 0, 1, HEAD_DIM ** -0.5),
    Unit("forget", 2, 0, HEAD_DIM ** -0.5),
]


def distance_tables(width):
    dist = np.arange(width) - (P - 1)
    n = np.maximum(dist, 0)
    exact = BUCKETS // 2
    big = np.log(np.maximum(n, 1) / exact) / np.log(MAX_DISTANCE / exact) * (BUCKETS - exact)
    bucket = np.where(n < exact, n, np.minimum(exact + big.astype(np.int64), BUCKETS - 1))
    pick = (np.arange(BUCKETS)[:, None] == bucket[None, :]).astype(np.float32)
    pick[BUCKETS - 1] -= 1.0
    mask = np.where(dist < 0, np.float32(NEG), np.float32(0.0))[None, :].repeat(UNITS, 0)
    return pick, np.ascontiguousarray(mask.astype(np.float32))


class Plan:

    def __init__(self, seq, k_tiles):
        self.nt = nt = seq // P
        self.k_tiles = k_tiles
        self.steps = [(t, i) for t in range(len(UNIT)) for i in range(nt)]
        self.n_steps = len(self.steps)
        self.chunks, self.t_chunks, self.last_chunk = {}, {}, {}
        self.first_chunk = {}
        n = tau = 0
        for g, (t, i) in enumerate(self.steps):
            kind = UNIT[t].kind
            self.first_chunk.setdefault(t, n)
            keys = 2 * P if kind == "mem" else (i + 1) * P
            cuts = [(c, min(BANK, keys - c)) for c in range(0, keys, BANK)]
            if kind == "stick":
                cuts.reverse()
            self.chunks[g] = []
            for m in range(2 if UNIT[t].has_k else 1):
                for c, w in cuts:
                    self.chunks[g].append((n, m, c, w))
                    n += 1
            self.last_chunk[t] = n
            self.t_chunks[g] = []
            for m in range(2 if kind in ("stick", "forget") else 1):
                for c, w in cuts:
                    self.t_chunks[g].append((tau, m, c // P, w // P))
                    tau += 1
        self.j = self.c = 0
        self.conv_of, self.job_of, self.gate_job, self.y_job = {}, {}, {}, {}
        self.clock = {"pe": 0.0, "act": 0.0, "dve": 0.0}
        self.at, self.script, self.open = {}, [], None
        self.order()

    def score_stream(self):
        for g in range(self.n_steps):
            todo, stick = self.chunks[g], UNIT[self.steps[g][0]].kind == "stick"
            for q in range(len(todo) + 1):
                if q < len(todo):
                    yield "scores", g, todo[q]
                if stick and q:
                    yield "log", g, todo[q - 1]

    def probs_stream(self):
        for g in range(self.n_steps):
            for m in sorted({ch[1] for ch in self.chunks[g]}):
                if UNIT[self.steps[g][0]].kind != "stick":
                    yield "peak", g, m
                for ch in self.chunks[g]:
                    if ch[1] == m:
                        yield "exp", g, ch

    def value_stream(self):
        for g in range(self.n_steps):
            todo, diff = self.t_chunks[g], UNIT[self.steps[g][0]].kind == "diff"
            if diff:
                yield "combine", g, todo[0]
            for q in range(len(todo) + MIX_LAG):
                if q < len(todo):
                    if diff and q + 1 < len(todo):
                        yield "combine", g, todo[q + 1]
                    yield "turn", g, todo[q]
                if q >= MIX_LAG:
                    r = q - MIX_LAG
                    yield "mix", g, todo[r], r == 0, r == len(todo) - 1

    def end_stream(self):
        for g in range(self.n_steps):
            yield "take", g
            if UNIT[self.steps[g][0]].kind == "diff":
                yield "variance", g
                yield "root", g
            yield "post", g
            yield "y", g

    def gate_stream(self):
        for g, (t, i) in enumerate(self.steps):
            if i == 0:
                yield "convert", (t, G)
            yield from self.project("g", t, G, g)
            yield "gate", g
            yield "silu", g

    def projection_stream(self):
        chunks = self.nt * P // BANK
        for c in range(chunks):
            yield from self.project("qk", 0, Q, c)
            yield "halves", ("qk", 0, Q, c)
        for t in range(1, len(UNIT)):
            yield "convert", (t, V)
            yield "convert", (t, Q)
            yield "convert", (t, K)
            wide = [("qk", t, kind, c) for c in range(chunks) for kind in (Q, K)]
            early = [("v", t, V, i) for i in range(self.nt)]
            own = EARLY_V[t] * self.nt // 16
            for q, job in enumerate(wide):
                yield from self.project(*job)
                yield "halves", job
                for v in early[q * own // len(wide):(q + 1) * own // len(wide)]:
                    yield from self.project(*v)
                    yield "halves", v
            for v in early[own:]:
                yield from self.project(*v)
                yield "halves", v
        yield "convert", (0, Q)

    def project(self, what, t, kind, index):
        step = 1 if what == "qk" else self.k_tiles // 2
        for k in range(0, self.k_tiles, step):
            yield "part", (what, t, kind, index), k, k + step

    def allowed(self, op):
        what, a = op[0], op[1]
        done = self.done
        if what in ("part", "halves") and (self.open or a) != a:
            return False
        if what == "y":
            return self.open is None
        if what == "scores":
            g, (n, m, c, w) = a, op[2]
            t, i = self.steps[g]
            return ("stacks", t, i // 4) in done and (g < 2 or ("step", g - 2) in done)
        if what == "peak":
            return ("chunk", self.last_of(a, op[2])) in done and (a < 2 or ("post", a - 2) in done)
        if what == "exp":
            return UNIT[self.steps[a][0]].kind != "stick" or ("log", op[2][0]) in done
        if what == "combine":
            return ("exp", self.last_of(a, 1)) in done
        if what == "turn":
            g, (tau, m, k0, tiles) = a, op[2]
            if UNIT[self.steps[g][0]].kind == "diff":
                return ("combine", tau) in done
            return ("exp", self.chunk_at(g, m, k0)) in done
        if what == "mix":
            t, i = self.steps[a]
            return (a == 0 or ("take", a - 1) in done) and (t == 0 or ("halves", ("v", t, V, i)) in done)
        if what == "take":
            return ("step", a) in done
        if what in ("variance", "post"):
            return ("silu", a) in done
        if what == "silu":
            return a == 0 or ("post", a - 1) in done
        if what == "part":
            kind, t = a[0], a[1]
            if kind == "v":
                return t < 2 or ("step", (t - 1) * self.nt - 1) in done
            if kind == "qk":
                return t < 2 or ("chunk", self.last_chunk[t - 2] - 1) in done
        return True

    def last_of(self, g, m):
        return max(ch[0] for ch in self.chunks[g] if ch[1] == m)

    def chunk_at(self, g, m, k0):
        return next(n for n, r, c, _ in self.chunks[g] if r == m and c == k0 * P)

    def estimate(self, op):
        clock, at, new, stall = dict(self.clock), self.at, {}, {"pe": 0.0, "act": 0.0, "dve": 0.0}

        def use(engine, length, *after):
            start = max([clock[engine]] + [new.get(k, at.get(k, 0.0)) + HOP for k in after])
            stall[engine] += start - clock[engine]
            clock[engine] = start + length
            return clock[engine]

        def act(w, sbuf=False):
            return (0.093 if sbuf else 0.052) + w * 0.00083

        def dve(w):
            return 0.069 + w * 0.00104

        what, a = op[0], op[1]
        kind = UNIT[self.steps[a][0]].kind if isinstance(a, int) else None
        if what == "scores":
            n, m, c, w = op[2]
            length = w * 0.00086 + {"stick": 0.03, "forget": w * 0.00043 + 0.03, "diff": 0.1, "mem": w * 0.00043}[kind]
            new["s_full", n] = use("pe", length, ("s_free", n - S_BANKS), ("stacks", *self.steps[a]))
            if kind == "stick":
                new["e", n] = use("act", act(w) + act(w, True) + 0.15, ("s_full", n))
            else:
                new["s_free", n] = use("dve", dve(w), ("s_full", n))
        elif what == "log":
            n, m, c, w = op[2]
            new["ln", n] = use("act", act(w, True), ("e", n))
            new["s_free", n] = use("dve", 3 * dve(w) + 0.3, ("ln", n))
        elif what == "peak":
            new["peak", a, op[2]] = use("dve", 0.07, ("s_free", self.last_of(a, op[2])))
        elif what == "exp":
            n, m, c, w = op[2]
            new["exp", n] = use("act", act(w, True), ("s_free", n) if kind == "stick" else ("peak", a, m))
        elif what == "combine":
            tau, m, k0, tiles = op[2]
            new["combine", tau] = use("dve", dve(tiles * P) + (0.9 if k0 == 0 else 0.0), ("exp", self.last_of(a, 1)))
        elif what == "turn":
            tau, m, k0, tiles = op[2]
            ready = ("combine", tau) if kind == "diff" else ("exp", self.chunk_at(a, m, k0))
            new["t_full", tau] = use("pe", tiles * 0.11, ("t_free", tau - T_BANKS), ready)
            new["t_hi", tau] = use("act", act(tiles * P), ("t_full", tau), ("pv", tau - PT_RING))
            new["t_free", tau] = use("dve", dve(tiles * P), ("t_hi", tau))
        elif what == "mix":
            tau, m, k0, tiles = op[2]
            each = 0.055 if kind in ("diff", "mem") else 0.035
            new["pv", tau] = use("pe", tiles * 3 * each, ("t_free", tau), ("take", a - 1),
                                 ("v", *self.steps[a]))
        elif what == "take":
            new["take", a] = use("act", act(P), ("pv", self.t_chunks[a][-1][0]), ("post", a - 1))
        elif what == "variance":
            new["variance", a] = use("dve", 1.3, ("take", a))
        elif what == "root":
            new["root", a] = use("act", 0.5, ("variance", a))
        elif what == "post":
            length = {"stick": 0.2, "forget": 0.85, "mem": 0.65, "diff": 1.2}[kind]
            new["post", a] = use("dve", length, ("take", a), ("root", a), ("silu", a))
        elif what == "part":
            job, k0, k1 = op[1:]
            each = 0.64 if job[0] == "qk" else 0.17
            unit = self.steps[job[3]][0] if job[0] == "g" else job[1]
            new["j_full"] = use("pe", each * (k1 - k0), ("w", unit, job[2]),
                                *([("j_free", self.j - J_BANKS)] if k0 == 0 else []))
        elif what == "gate":
            new["j_free", self.j - 1] = use("dve", dve(P), "j_full")
            new["gate", a] = use("act", act(P, True), ("j_free", self.j - 1))
        elif what == "silu":
            new["sig", a] = use("act", 2 * act(P, True) + 0.15, ("gate", a))
            new["silu", a] = use("dve", dve(P), ("sig", a))
        elif what == "halves":
            w = BANK if a[0] == "qk" else P
            new["j_hi"] = use("act", act(w), "j_full")
            new["j_free", self.j - 1] = new[a[0], a[1], a[3]] = use("dve", dve(w), "j_hi")
        elif what == "y":
            new["y"] = use("pe", 0.12, ("post", a), ("j_free", self.j - J_BANKS))
            new["y"] = use("act", act(P), "y")
            new["j_free", self.j] = use("dve", dve(P), "y")
        elif what == "convert":
            n = self.c
            landed = max(at.get(("strip", n - 1), 0.0), at.get(("w", n - 2), 0.0)) + 5.0
            new["strip", n] = landed
            new["hi"] = use("act", 0.95, ("strip", n))
            new["w", n] = new["w", a[0], a[1]] = use("dve", 1.15, "hi")
        return clock, new, stall

    def order(self):
        streams = {"end": self.end_stream(), "value": self.value_stream(), "probs": self.probs_stream(),
                   "score": self.score_stream(), "gate": self.gate_stream(),
                   "project": self.projection_stream()}
        heads = {name: next(s) for name, s in streams.items()}
        self.done = set()
        jobs_done, unit_jobs = 0.0, 0
        while heads:
            best = None
            for name, op in heads.items():
                if not self.allowed(op):
                    continue
                clock, new, stall = self.estimate(op)
                cost = stall["pe"] + STALL_W * (stall["act"] + stall["dve"]) + BIAS[name]
                if name == "project":
                    t = op[1][1] if op[0] in ("part", "halves") else op[1][0]
                    if t:
                        cost += PACE * (jobs_done - self.target(t))
                if best is None or cost < best[0]:
                    best = (cost, name, op, clock, new)
            _, name, op, clock, new = best
            self.clock = clock
            self.at.update(new)
            self.emit(op)
            if name == "project":
                t = op[1][1] if op[0] in ("part", "halves") else op[1][0]
                if t != unit_jobs:
                    unit_jobs, jobs_done = t, 0.0
                if op[0] == "part":
                    jobs_done += (op[3] - op[2]) * (0.64 if op[1][0] == "qk" else 0.17)
            heads[name] = next(streams[name], None)
            if heads[name] is None:
                del heads[name]

    def target(self, t):
        first, last = self.first_chunk[t - 1], self.last_chunk[t - 1]
        whole = [w + 100 for g in range(self.n_steps) if self.steps[g][0] == t - 1 for _, _, _, w in self.chunks[g]]
        now = sum(w for n, w in zip(range(first, last), whole) if ("chunk", n) in self.done)
        return 1.02 * now / sum(whole) * (2 * self.nt * P // BANK * 5.2 + EARLY_V[t] * self.nt / 16 * 1.36)

    def emit(self, op):
        what, a = op[0], op[1]
        done = self.done
        if what == "convert":
            self.conv_of[a] = self.c
            op = ("convert", (self.c, *a))
            self.c += 1
        elif what == "part":
            if op[2] == 0:
                self.job_of[a] = (self.j, *a)
                self.j += 1
                if a[0] == "g":
                    self.gate_job[a[3]] = self.job_of[a]
            self.open = a
            op = ("part", self.job_of[a], *op[2:])
        elif what == "halves":
            self.open = None
            op = ("halves", self.job_of[a])
        elif what == "gate":
            self.open = None
        elif what == "y":
            self.y_job[a] = (self.j, "y", None, None, a)
            self.j += 1
        elif what == "scores":
            done.add(("chunk", op[2][0]))
        elif what == "log":
            done.add(("log", op[2][0]))
        elif what == "mix":
            if op[4]:
                done.add(("step", a))
        elif what == "combine":
            done.add(("combine", op[2][0]))
        if what == "exp":
            done.add(("exp", op[2][0]))
        elif what == "halves":
            done.add(("halves", a))
        else:
            done.add((what, a))
        self.script.append(op)
        if what == "y" and a % 4 == 3:
            self.script.append(("store", a))
        if what == "log" and op[2][0] == self.last_chunk[self.steps[a][0]] - 1:
            self.script.append(("sums", a))
        for t in range(len(UNIT)):
            for c in range(self.nt * P // BANK):
                kinds = (Q, K) if UNIT[t].has_k else (Q,)
                if ("stacks", t, c) not in done and all(("halves", ("qk", t, kind, c)) in done for kind in kinds) \
                        and (t == 0 or ("chunk", self.last_chunk[t - 1] - 1) in done):
                    done.add(("stacks", t, c))
                    ready = max(self.clock.values()) + 5.0
                    for i in range(4 * c, min(4 * c + 4, self.nt)):
                        self.at["stacks", t, i] = ready
                    self.script.append(("stacks", t, c))


def build(nc, x, mem, w_in, b_forget, w_mem_kv, w_out, pre_norm, post_norm, mem_norm,
          diff_lambda, diff_head_norm, rel_bias, pick, dmask, out):
    _, SEQ, D = x.shape
    KT = D // P
    NT = SEQ // P
    NC = SEQ // BANK
    D_MIX = w_out.shape[1]
    YT = D_MIX // P
    MEM_T = mem.shape[1] // P
    MEM_LEN = mem.shape[1]
    DIST_W = pick.shape[1]
    plan = Plan(SEQ, KT)
    assert D == KT * P and MEM_T == 2 and KT * P <= 1024

    y_dram = nc.dram_tensor("y_halves", (2, D_MIX, SEQ), F16, kind="Internal").ap()
    c_dram = nc.dram_tensor("forget_parts", (3, HEADS_FOX, SEQ), BF16, kind="Internal").ap()
    dist_dram = nc.dram_tensor("bias_by_distance", (UNITS, DIST_W), F32, kind="Internal").ap()
    near_dram = nc.dram_tensor("near_bias", (UNITS, P, 2 * P), F32, kind="Internal").ap()
    km_dram = nc.dram_tensor("mem_keys", (UNITS, P, 2, MEM_LEN), F16, kind="Internal").ap()
    vm_dram = nc.dram_tensor("mem_values", (MEM_T, UNITS, P, 2, P), F16, kind="Internal").ap()

    w_cols = w_in[0].rearrange("(k p) n -> p k n", p=P)
    w_mem_cols = w_mem_kv[0].rearrange("(k p) n -> p k n", p=P)
    w_out_rows = w_out[0].rearrange("(k p) n -> k p n", p=P)

    with ExitStack() as ctx:
        def sb(name, shape, dt):
            return ctx.enter_context(nc.sbuf_tensor(name, shape, dt))

        def sem(name):
            return ctx.enter_context(nc.semaphore(name))

        s_bank = [ctx.enter_context(nc.psum_tensor(f"scores{b}", [P, BANK], F32)) for b in range(S_BANKS)]
        t_bank = [ctx.enter_context(nc.psum_tensor(f"turned{b}", [P, BANK], F32)) for b in range(T_BANKS)]
        j_bank = [ctx.enter_context(nc.psum_tensor(f"job{b}", [P, BANK], F32)) for b in range(J_BANKS)]
        o_bank = ctx.enter_context(nc.psum_tensor("mixed", [P, BANK], F32))

        big = sb("big", [P, max(2 * KT * SEQ, 2 * YT * D)], F16)
        hT = big[:, 0:2 * KT * SEQ].rearrange("p (h k s) -> p h k s", h=2, k=KT)
        wo = big[:, 0:2 * YT * D].rearrange("p (h k n) -> p h k n", h=2, k=YT)
        st_len = max(6 * SEQ, 5 * 2 * D)
        stack_flat = sb("stack", [P, st_len], F16)
        stack = stack_flat[:, 0:6 * SEQ].rearrange("p (a s) -> p a s", a=6)
        planes = sb("planes", [P, 4, max(SEQ, KT * MEM_LEN)], F16)
        values = [sb(f"values{b}", [P, NT, 2, P], F16) for b in range(2)]
        rows_flat = sb("rows", [P, ROWS * max(SEQ, 2048)], F32)
        rows = rows_flat[:, 0:ROWS * max(SEQ, 2048)].rearrange("p (r s) -> p r s", r=ROWS)
        ws = sb("ws", [P, 2, KT * P], F32)
        wt = sb("wt", [P, 4, 2, KT, P], F16)
        turned = sb("turned_halves", [P, PT_RING, 2, BANK], F16)
        temps = sb("temps", [P, max(5 * BANK, SEQ)], F32)
        e_buf = [temps[:, b * BANK:(b + 1) * BANK] for b in range(3)]
        c_buf = [temps[:, (3 + b) * BANK:(4 + b) * BANK] for b in range(2)]
        c_rows = temps[0:3, 0:SEQ].bitcast(BF16).rearrange("p (h s) -> p h s", h=2)
        ident = sb("ident", [P, P], F32)
        ident_b = sb("ident_b", [P, P], BF16)
        strict = sb("strict", [P, P], BF16)
        causal = sb("causal", [P, P], BF16)
        near_f = sb("near_f", [P, 2 * P], F32)
        near = sb("near", [P, 3, 2 * P], BF16)
        ones3 = sb("ones3", [3, P], BF16)
        neg_lam = sb("neg_lam", [P, 1], F32)
        head_gain = sb("head_gain", [P, P], F32)
        y_halves = sb("y_out_halves", [P, 2, 2, BANK], F16)
        gate_e = sb("gate_e", [P, P], F32)
        gate_f = sb("gate_f", [P, P], F32)
        gate_s = sb("gate_s", [P, P], F32)
        o_copy = sb("o_copy", [P, P], F32)
        junk = sb("junk", [P, P], F32)
        y_f = sb("y_f", [P, 2, P], F32)
        mx = sb("mx", [P, ROWS, 4], F32)
        neg_max = sb("neg_max", [P, ROWS], F32)
        z_sum = sb("z_sum", [P, ROWS], F32)
        z_part = sb("z_part", [P, ROWS, 4], F32)
        rz = sb("rz", [P, 2], F32)
        sc = sb("sc", [P, 16], F32)
        gain = sb("gain", [P, 2, KT], F32)
        eps = sb("eps", [P, 1], F32)
        one = sb("one", [P, 1], F32)

        TILES = MEM_T + NT
        x_in = [rows[:, 0, 0:D], rows[:, 0, D:2 * D], rows[:, 1, 0:D]]
        x_n = [rows[:, 1, D:2 * D], rows[:, 2, 0:D]]
        x_g = [rows[:, 2, D:2 * D], rows[:, 3, 0:D]]
        tile_banks = [(s_bank[0], s_bank[1]), (t_bank[0], t_bank[1])]
        memT = planes[:, 0:2, 0:KT * MEM_LEN].rearrange("p h (k s) -> p h k s", k=KT)
        HALF = KT // 2
        km_sb = values[1][:, 0:4].rearrange("p a b c -> p (a b c)").rearrange("p (h s) -> p h s", h=2)
        vm_sb = values[0][:, 0:1].rearrange("p a b c -> p (a b) c")
        f_w = turned[:, 0].rearrange("p a b -> p (a b)")[:, 0:2 * KT * HEADS_FOX] \
            .rearrange("p (h k n) -> p h k n", h=2, k=KT)
        f_wf = junk[:, 0:KT * HEADS_FOX]
        pick_sb = stack_flat[0:BUCKETS, 0:2 * DIST_W].bitcast(F32)
        dmask_sb = stack_flat[0:UNITS, 2 * DIST_W:4 * DIST_W].bitcast(F32)
        rel_sb = stack_flat[0:BUCKETS, 4 * DIST_W:4 * DIST_W + 2 * UNITS].bitcast(F32)
        dist_sb = stack_flat[0:UNITS, 4 * DIST_W + 16:6 * DIST_W + 16].bitcast(F32)
        lam_sb = stack_flat[:, 6 * DIST_W + 16:6 * DIST_W + 16 + 8 * HEAD_DIM].bitcast(F32)
        b_sb = sc[0:HEADS_FOX, 15:16]
        fl = [rows[0:HEADS_FOX, r, 0:SEQ] for r in range(4)]
        parts_at = 6 * DIST_W + 16 + 8 * HEAD_DIM
        c_parts = stack_flat[0:HEADS_FOX, parts_at:parts_at + 3 * SEQ].bitcast(BF16) \
            .rearrange("p (a s) -> p a s", a=3)

        tile_in = [sem(f"tile_in{b}") for b in range(3)]
        consts_in, pool_made, consts_made = sem("consts_in"), sem("pool_made"), sem("consts_made")
        root_ready, norm_step, tile_n, tile_t, tile_g, tile_hi, tile_done = (
            sem(n) for n in ("root_ready", "norm_step", "tile_n", "tile_t", "tile_g", "tile_hi", "tile_done"))
        mw_in = [sem(f"mw_in{b}") for b in range(2)]
        mw_hi, mw_ready, mj_full, mj_hi, mj_done = (
            sem(n) for n in ("mw_hi", "mw_ready", "mj_full", "mj_hi", "mj_done"))
        m_stored = [sem(f"m_stored{b}") for b in range(2)]
        f_full, f_step, f_act, lam_step, lam_exp, lam_done, pre_stored, dist_full, dist_ready, near_stored = (
            sem(n) for n in ("f_full", "f_step", "f_act", "lam_step", "lam_exp", "lam_done", "pre_stored",
                             "dist_full", "dist_ready", "near_stored"))
        F_STEPS = NC + 8
        assert 2 * UNITS % 4 == Q
        MEM_JOBS = [(s, t) for s in range(2 * UNITS) for t in ((0,) if s < UNITS else range(MEM_T))]

        def mem_count(s):
            return 1 if s < UNITS else MEM_T

        def mem_first(s):
            return sum(mem_count(r) for r in range(s))

        def km_view(n):
            return km_sb[:, :, (n % 2) * MEM_LEN:(n % 2 + 1) * MEM_LEN]

        def vm_view(n):
            return values[0][:, n % 4]

        def mem_out(n):
            s, t = MEM_JOBS[n]
            if s < UNITS:
                return j_bank[n % 2][:, 0:MEM_LEN], km_view(n)
            return j_bank[n % 2][:, 0:P], vm_view(n)

        def mem_high(act, n):
            act.wait_ge(mj_full, n + 1)
            if n >= 2:
                act.wait_ge(m_stored[n % 2], 16 * (n // 2))
            src, dst = mem_out(n)
            nc.scalar.activation(dst[:, 0], src, ACT.Copy, scale=1.0 / W_SCALE).then_inc(mj_hi, 1)

        def mem_low(dve, n):
            dve.wait_ge(mj_hi, n + 1)
            src, dst = mem_out(n)
            nc.vector.scalar_tensor_tensor(dst[:, 1], src, 1.0 / W_SCALE, dst[:, 0], op0=ALU.mult,
                                           op1=ALU.subtract).then_inc(mj_done, 1)

        def junk_lam(a):
            return y_f[:, a, 0:HEAD_DIM]

        with nc.Block() as block:
            @block.sync
            def _(sp):
                def load_tile(a):
                    src = mem[0, a * P:(a + 1) * P, :] if a < MEM_T else x[0, (a - MEM_T) * P:(a - MEM_T + 1) * P, :]
                    if a >= 3:
                        sp.wait_ge(tile_n, a - 2)
                    sp.dma_start(x_in[a % 3], src).then_inc(tile_in[a % 3], 16)

                for a in range(3):
                    load_tile(a)
                sp.dma_start(gain[:, 0, :], mem_norm[0].rearrange("(k p) -> p k", p=P), allow_slow_non_contiguous=True).then_inc(consts_in, 16)
                sp.dma_start(gain[:, 1, :], pre_norm[0].rearrange("(k p) -> p k", p=P), allow_slow_non_contiguous=True).then_inc(consts_in, 16)
                sp.dma_start(b_sb, b_forget[0].rearrange("(h a) -> h a", a=1)).then_inc(consts_in, 16)
                sp.dma_start(pick_sb, pick).then_inc(consts_in, 16)
                sp.dma_start(dmask_sb, dmask).then_inc(consts_in, 16)
                sp.dma_start(rel_sb, rel_bias).then_inc(consts_in, 16)
                sp.dma_start(lam_sb, diff_lambda[0].rearrange("a d -> (a d)").partition_broadcast(P)) \
                    .then_inc(consts_in, 16)
                sp.dma_start(head_gain[:, :], diff_head_norm[0].partition_broadcast(P)).then_inc(consts_in, 16)
                sp.dma_start(f_wf.rearrange("p (k n) -> p k n", k=KT),
                             w_cols[:, :, COL_FORGET:COL_FORGET + HEADS_FOX]).then_inc(consts_in, 16)
                for a in range(3, TILES):
                    load_tile(a)
                for s in range(2 * UNITS + 1):
                    if s >= 2:
                        sp.wait_ge(mw_ready, s - 1)
                    src = w_mem_cols[:, :, s * P:(s + 1) * P] if s < 2 * UNITS else \
                        w_cols[:, :, UNIT[0].col[Q]:UNIT[0].col[Q] + P]
                    sp.dma_start(ws[:, s % 2, :].rearrange("p (k n) -> p k n", k=KT), src) \
                        .then_inc(mw_in[s % 2], 16)
                sp.wait_ge(dist_ready, 1)
                sp.dma_start(dist_dram, dist_sb).then_inc(near_stored, 16)
                sp.wait_ge(near_stored, 16)
                for h in range(UNITS):
                    sp.dma_start(near_dram[h], bass.AP(dist_dram.tensor, h * DIST_W, [[1, P], [1, 2 * P]])) \
                        .then_inc(pre_stored, 16)
                sp.wait_ge(f_step, F_STEPS)
                for part in range(3):
                    sp.dma_start(c_dram[part], c_parts[:, part, :]).then_inc(pre_stored, 16)
                for b in range(2):
                    sp.wait_ge(m_stored[b], 16 * len(MEM_JOBS) // 2)
                sp.wait_ge(pre_stored, 16 * (3 + UNITS))

            @block.gpsimd
            def _(pool):
                nc.gpsimd.memset(ident[:, :], 0.0).then_inc(pool_made, 1)
                nc.gpsimd.memset(o_copy[:, :], 0.0).then_inc(pool_made, 1)
                nc.gpsimd.memset(gate_e[:, :], 0.0).then_inc(pool_made, 1)
                pool.wait_ge(pool_made, 3)
                nc.gpsimd.affine_select(out=ident[:, :], in_=ident[:, :], compare_op=ALU.not_equal, fill=1.0,
                                        base=0, pattern=[[-1, P]], channel_multiplier=1).then_inc(pool_made, 1)
                nc.gpsimd.affine_select(out=o_copy[:, :], in_=o_copy[:, :], compare_op=ALU.is_gt, fill=NEG,
                                        base=0, pattern=[[-1, P]], channel_multiplier=1).then_inc(pool_made, 1)
                nc.gpsimd.affine_select(out=gate_e[:, :], in_=gate_e[:, :], compare_op=ALU.is_ge, fill=NEG,
                                        base=0, pattern=[[-1, P]], channel_multiplier=1).then_inc(pool_made, 1)
                for n, (s, t) in enumerate(MEM_JOBS):
                    pool.wait_ge(mj_done, n + 1)
                    if s < UNITS:
                        pool.dma_start(km_dram[s], km_view(n)).then_inc(m_stored[n % 2], 16)
                    else:
                        pool.dma_start(vm_dram[t, s - UNITS], vm_view(n)).then_inc(m_stored[n % 2], 16)

            @block.scalar
            def _(act):
                nc.scalar.preload_act_table_set("natural_log_exp_and_others")
                act.wait_ge(consts_made, 6)

                def root(a):
                    act.wait_ge(tile_in[a % 3], 16 * (a // 3 + 1))
                    if a >= 2:
                        act.wait_ge(tile_t, a - 1)
                    nc.scalar.activation(x_n[a % 2], x_in[a % 3], ACT.Square,
                                         accum_out=sc[:, a % 2:a % 2 + 1]).then_inc(norm_step, 1)
                    act.wait_ge(norm_step, 3 * a + 1)
                    nc.scalar.activation(sc[:, 2 + a % 2:3 + a % 2], sc[:, a % 2:a % 2 + 1], ACT.Ln,
                                         scale=1.0 / D, bias=eps[:, :]).then_inc(norm_step, 1)
                    act.wait_ge(norm_step, 3 * a + 2)
                    nc.scalar.activation(sc[:, 4 + a % 2:5 + a % 2], sc[:, 2 + a % 2:3 + a % 2], ACT.Exp,
                                         scale=-0.5).then_inc(norm_step, 1)

                def high(a):
                    act.wait_ge(tile_g, 2 * a + 2)
                    if a < MEM_T:
                        dst = memT[:, 0, :, a * P:(a + 1) * P]
                    else:
                        dst = hT[:, 0, :, (a - MEM_T) * P:(a - MEM_T + 1) * P]
                    nc.scalar.copy(dst, x_g[a % 2].rearrange("p (k s) -> p k s", k=KT)).then_inc(tile_hi, 1)

                for a in range(TILES):
                    root(a)
                    if a >= 1:
                        high(a - 1)
                high(TILES - 1)
                act.wait_ge(lam_step, 2)
                nc.scalar.activation(sc[:, 12:14], sc[:, 10:12], ACT.Exp).then_inc(lam_exp, 1)
                n = 0
                for s in range(2 * UNITS + 1):
                    act.wait_ge(mw_in[s % 2], 16 * (s // 2 + 1))
                    if s >= 4:
                        act.wait_ge(mj_full, mem_first(s - 3))
                    nc.scalar.activation(wt[:, s % 4, 0], ws[:, s % 2, :].rearrange("p (k n) -> p k n", k=KT),
                                         ACT.Copy, scale=W_SCALE).then_inc(mw_hi, 1)
                    if s == 2:
                        act.wait_ge(f_step, NC + 1)
                        nc.scalar.activation(fl[1], fl[1], ACT.Exp, scale=-1.0).then_inc(f_act, 1)
                        act.wait_ge(f_act, 1)
                        nc.scalar.activation(fl[1], fl[1], ACT.Ln, bias=one[0:HEADS_FOX, :]).then_inc(f_act, 1)
                    if s >= 1:
                        for _ in range(mem_count(s - 1)):
                            mem_high(act, n)
                            n += 1

            @block.vector
            def _(dve):
                nc.vector.memset(eps[:, :], EPS).then_inc(consts_made, 1)
                nc.vector.memset(one[:, :], 1.0).then_inc(consts_made, 1)
                nc.vector.memset(ones3[:, :], 1.0).then_inc(consts_made, 1)
                dve.wait_ge(pool_made, 6)
                nc.vector.tensor_copy(ident_b[:, :], ident[:, :]).then_inc(consts_made, 1)
                nc.vector.tensor_copy(strict[:, :], o_copy[:, :]).then_inc(consts_made, 1)
                nc.vector.tensor_copy(causal[:, :], gate_e[:, :]).then_inc(consts_made, 1)
                dve.wait_ge(consts_in, 16 * 9)
                nc.vector.tensor_scalar(head_gain[:, :], head_gain[:, :], 1.0 - LAM_INIT, None, ALU.mult) \
                    .then_inc(consts_made, 1)
                nc.vector.tensor_scalar(f_w[:, 0], f_wf.rearrange("p (k n) -> p k n", k=KT), W_SCALE, None,
                                        ALU.mult).then_inc(consts_made, 1)
                dve.wait_ge(consts_made, 8)
                nc.vector.scalar_tensor_tensor(f_w[:, 1], f_wf.rearrange("p (k n) -> p k n", k=KT), W_SCALE,
                                               f_w[:, 0], op0=ALU.mult, op1=ALU.subtract).then_inc(consts_made, 1)
                for a in range(2):
                    nc.vector.tensor_tensor_reduce(
                        out=junk_lam(a), in0=lam_sb[:, 2 * a * HEAD_DIM:(2 * a + 1) * HEAD_DIM],
                        in1=lam_sb[:, (2 * a + 1) * HEAD_DIM:(2 * a + 2) * HEAD_DIM], scale=1.0, scalar=0.0,
                        op0=ALU.mult, op1=ALU.add, accum_out=sc[:, 10 + a:11 + a]).then_inc(lam_step, 1)

                def norm(a):
                    s0, r0, v, h = (sc[:, c + a % 2:c + a % 2 + 1] for c in (0, 4, 6, 8))
                    dve.wait_ge(norm_step, 3 * a + 3)
                    nc.vector.tensor_scalar(v, s0, 1.0 / D, EPS, ALU.mult, ALU.add).then_inc(root_ready, 1)
                    dve.wait_ge(root_ready, 4 * a + 1)
                    nc.vector.tensor_scalar(v, v, r0, r0, ALU.mult, ALU.mult).then_inc(root_ready, 1)
                    dve.wait_ge(root_ready, 4 * a + 2)
                    nc.vector.tensor_scalar(v, v, -0.5, 1.5, ALU.mult, ALU.add).then_inc(root_ready, 1)
                    dve.wait_ge(root_ready, 4 * a + 3)
                    nc.vector.tensor_tensor(h, v, r0, ALU.mult).then_inc(root_ready, 1)
                    dve.wait_ge(root_ready, 4 * a + 4)
                    nc.vector.tensor_scalar(x_n[a % 2], x_in[a % 3], h, None, ALU.mult).then_inc(tile_n, 1)

                def gained(a):
                    dve.wait_ge(tile_t, a + 1)
                    for b in range(2):
                        g = gain[:, 0 if a < MEM_T else 1, b * HALF:(b + 1) * HALF]
                        nc.vector.tensor_tensor(
                            x_g[a % 2][:, b * HALF * P:(b + 1) * HALF * P].rearrange("p (k s) -> p k s", k=HALF),
                            tile_banks[a % 2][b][:, :].rearrange("p (k s) -> p k s", k=HALF),
                            g.unsqueeze(2).to_broadcast([P, HALF, P]), ALU.mult).then_inc(tile_g, 1)
                    dve.wait_ge(tile_hi, a + 1)
                    if a < MEM_T:
                        dst = memT[:, :, :, a * P:(a + 1) * P]
                    else:
                        dst = hT[:, :, :, (a - MEM_T) * P:(a - MEM_T + 1) * P]
                    nc.vector.tensor_tensor(dst[:, 1], x_g[a % 2].rearrange("p (k s) -> p k s", k=KT), dst[:, 0],
                                            ALU.subtract).then_inc(tile_done, 1)

                def forget_gates(s):
                    if s == 1:
                        for c in range(NC):
                            dve.wait_ge(f_full, c + 1)
                            nc.vector.tensor_scalar(fl[0][:, c * BANK:(c + 1) * BANK], s_bank[c % 2][0:HEADS_FOX, :],
                                                    1.0 / W_SCALE, b_sb, ALU.mult, ALU.add).then_inc(f_step, 1)
                        dve.wait_ge(f_step, NC)
                        nc.vector.scalar_tensor_tensor(fl[1], fl[0], -1.0, fl[0], op0=ALU.mult, op1=ALU.max) \
                            .then_inc(f_step, 1)
                    if s == 3:
                        dve.wait_ge(f_act, 2)
                        nc.vector.scalar_tensor_tensor(fl[1], fl[0], 0.0, fl[1], op0=ALU.min,
                                                       op1=ALU.subtract).then_inc(f_step, 1)
                        dve.wait_ge(f_step, NC + 2)
                        nc.vector.tensor_tensor_scan(out=fl[2], data0=fl[1], data1=fl[1], initial=0.0, op0=ALU.add,
                                                     op1=ALU.bypass).then_inc(f_step, 1)
                    if s == 4:
                        dve.wait_ge(f_step, NC + 3)
                        nc.vector.tensor_scalar(c_parts[:, 0], fl[2], -1.0, None, ALU.mult).then_inc(f_step, 1)
                        dve.wait_ge(f_step, NC + 4)
                        nc.vector.scalar_tensor_tensor(fl[3], fl[2], -1.0, c_parts[:, 0], op0=ALU.mult,
                                                       op1=ALU.subtract).then_inc(f_step, 1)
                    if s == 5:
                        dve.wait_ge(f_step, NC + 5)
                        nc.vector.tensor_copy(c_parts[:, 1], fl[3]).then_inc(f_step, 1)
                    if s == 6:
                        dve.wait_ge(f_step, NC + 6)
                        nc.vector.tensor_tensor(fl[3], fl[3], c_parts[:, 1], ALU.subtract).then_inc(f_step, 1)
                        dve.wait_ge(f_step, NC + 7)
                        nc.vector.tensor_copy(c_parts[:, 2], fl[3]).then_inc(f_step, 1)

                for a in range(TILES):
                    norm(a)
                    if a >= 1:
                        gained(a - 1)
                gained(TILES - 1)
                dve.wait_ge(lam_exp, 1)
                nc.vector.tensor_tensor(sc[:, 14:15], sc[:, 13:14], sc[:, 12:13], ALU.subtract).then_inc(lam_done, 1)
                dve.wait_ge(lam_done, 1)
                nc.vector.tensor_scalar(neg_lam[:, :], sc[:, 14:15], -LAM_INIT, None, ALU.add).then_inc(lam_done, 1)
                dve.wait_ge(dist_full, 1)
                nc.vector.tensor_tensor(dist_sb, t_bank[0][0:UNITS, 0:DIST_W], dmask_sb, ALU.add) \
                    .then_inc(dist_ready, 1)
                n = 0
                for s in range(2 * UNITS + 1):
                    dve.wait_ge(mw_hi, s + 1)
                    nc.vector.scalar_tensor_tensor(
                        wt[:, s % 4, 1], ws[:, s % 2, :].rearrange("p (k n) -> p k n", k=KT), W_SCALE,
                        wt[:, s % 4, 0], op0=ALU.mult, op1=ALU.subtract).then_inc(mw_ready, 1)
                    forget_gates(s)
                    if s >= 1:
                        for _ in range(mem_count(s - 1)):
                            mem_low(dve, n)
                            n += 1

            @block.tensor
            def _(pe):
                pe.wait_ge(pool_made, 6)
                for a in range(TILES):
                    pe.wait_ge(tile_n, a + 1)
                    if a >= 2:
                        pe.wait_ge(tile_g, 2 * a - 2)
                    for k in range(KT):
                        last = nc.tensor.transpose(
                            tile_banks[a % 2][k // HALF][:, (k % HALF) * P:(k % HALF + 1) * P],
                            x_n[a % 2][:, k * P:(k + 1) * P], ident[:, :])
                    last.then_inc(tile_t, 1)
                pe.wait_ge(consts_in, 16 * 9)
                pe.wait_ge(tile_g, 2 * TILES)
                nc.tensor.matmul(t_bank[0][0:UNITS, 0:DIST_W], rel_sb, pick_sb, start=True, stop=True) \
                    .then_inc(dist_full, 1)
                pe.wait_ge(tile_done, TILES)
                for c in range(NC):
                    if c >= 2:
                        pe.wait_ge(f_step, c - 1)
                    for k in range(KT):
                        for a, b in ((0, 0), (0, 1), (1, 0)):
                            last = nc.tensor.matmul(
                                s_bank[c % 2][0:HEADS_FOX, :], f_w[:, a, k, :],
                                hT[:, b, k, c * BANK:(c + 1) * BANK], start=(k == 0 and a == b == 0),
                                stop=(k == KT - 1 and a == 1))
                    last.then_inc(f_full, 1)
                for n, (s, t) in enumerate(MEM_JOBS):
                    pe.wait_ge(mw_ready, s + 1)
                    if n >= 2:
                        pe.wait_ge(mj_done, n - 1)
                    dst, _ = mem_out(n)
                    w = wt[:, s % 4]
                    for k in range(KT):
                        for a, b in ((0, 0), (0, 1), (1, 0)):
                            if s < UNITS:
                                lhs, rhs = w[:, a, k, :], memT[:, b, k, :]
                            else:
                                lhs, rhs = memT[:, a, k, t * P:(t + 1) * P], w[:, b, k, :]
                            last = nc.tensor.matmul(dst, lhs, rhs, start=(k == 0 and a == b == 0),
                                                    stop=(k == KT - 1 and a == 1))
                    last.then_inc(mj_full, 1)

        s_full, s_free, stick_e, stick_abs, stick_ln, stick_sp, stick_sum = (
            sem(n) for n in ("s_full", "s_free", "stick_e", "stick_abs", "stick_ln", "stick_sp", "stick_sum"))
        max_ready, coef_step, combined, probs_ready = (
            sem(n) for n in ("max_ready", "coef_step", "combined", "probs_ready"))
        t_full, t_hi, t_free, pv_done, o_copied = (
            sem(n) for n in ("t_full", "t_hi", "t_free", "pv_done", "o_copied"))
        j_full, j_hi, j_free = (sem(n) for n in ("j_full", "j_hi", "j_free"))
        gate_exp, gate_done, gate_ln, var_ready, var_ln, root_done, post_step = (
            sem(n) for n in ("gate_exp", "gate_done", "gate_ln", "var_ready", "var_ln", "root_done", "post_step"))
        y_stored = [sem(f"y_stored{b}") for b in range(2)]
        w_in_sem = [sem(f"w_landed{b}") for b in range(2)]
        w_hi, w_ready = sem("w_hi"), sem("w_ready")
        stacked = [sem(f"stacked{c}") for c in range(NC)]
        c_landed, near_landed, near_step, mem_landed = (
            sem(n) for n in ("c_landed", "near_landed", "near_step", "mem_landed"))
        loop_sems = [s_full, s_free, stick_e, stick_abs, stick_ln, stick_sp, stick_sum, max_ready,
                     coef_step, combined, probs_ready, t_full, t_hi, t_free, pv_done, o_copied, j_full, j_hi, j_free, gate_exp,
                     gate_done, gate_ln, var_ready, var_ln, root_done, post_step, *y_stored, *w_in_sem, w_hi,
                     w_ready, *stacked, c_landed, near_landed, near_step, mem_landed]

        N_G = plan.n_steps
        KINDS = [UNIT[t].kind for t, _ in plan.steps]
        SOFT = [g for g in range(N_G) if KINDS[g] != "stick"]
        ROW_OF = {}
        for g in SOFT:
            for m in range(2 if KINDS[g] in ("forget", "diff") else 1):
                ROW_OF[g, m] = len(ROW_OF)
        DIFF_STEP = {g: n for n, g in enumerate([g for g in range(N_G) if KINDS[g] == "diff"])}
        DIFF_TAU = min(tau for g in DIFF_STEP for tau, _, _, _ in plan.t_chunks[g])
        STACKED = [16 + 64 * t for t in range(len(UNIT))]
        COEF = 4
        POST = {"stick": 1, "forget": 3, "mem": 3, "diff": 9}
        POST_AT, total = {}, 0
        for g in range(N_G):
            POST_AT[g] = total
            total += POST[KINDS[g]]
        Y_GROUPS = N_G // 4
        STORE = 16
        STICK = next(t for t, u in enumerate(UNIT) if u.kind == "stick")
        KM = values[1][:, 2:4].rearrange("p a b c -> p (a b c)").rearrange("p (h s) -> p h s", h=2)

        def row(g, m):
            return rows[:, (2 * g + m) % ROWS, :]

        def col(g, m):
            return slice((2 * g + m) % ROWS, (2 * g + m) % ROWS + 1)

        def mixed(g):
            return plan.t_chunks[g][-1][0] + 1

        def last_group_job(t, c):
            return plan.job_of["qk", t, K if UNIT[t].has_k else Q, c][0]

        def job_out(j):
            n, what, t, kind, index = j
            bank = j_bank[n % J_BANKS]
            if what == "qk":
                scale = (UNIT[t].scale if kind == Q else 1.0) / W_SCALE
                hi, lo = (HQ, LQ) if kind == Q else (HK, LK)
                at = slice(index * BANK, (index + 1) * BANK)
                return bank[:, :], planes[:, hi, at], planes[:, lo, at], scale
            if what == "v":
                v = values[UNIT[t].slot][:, index]
                return bank[:, 0:P], v[:, 0], v[:, 1], 1.0 / W_SCALE
            if what == "g":
                return bank[:, 0:P], None, None, 1.0 / W_SCALE
            at = slice(index % 4 * P, (index % 4 + 1) * P)
            y = y_halves[:, index // 4 % 2]
            return bank[:, 0:P], y[:, 0, at], y[:, 1, at], 1.0

        with nc.Fori(0, UNITS) as it:
            with nc.Block() as block:
                @block.sync
                def _(sp):
                    def load_weights(c):
                        n, t, kind = c
                        if n >= 2:
                            sp.wait_ge(w_ready, n - 1)
                        ahead = P if (t, kind) == (0, Q) else 0
                        sp.dma_start(ws[:, n % 2, :].rearrange("p (k n) -> p k n", k=KT),
                                     w_cols[:, :, bass.ds(UNIT[t].col[kind] + ahead + it * P, P)]) \
                            .then_inc(w_in_sem[n % 2], 16)

                    every = [op[1] for op in plan.script if op[0] == "convert"]
                    issued = 0

                    def load_up_to(n):
                        nonlocal issued
                        while issued < min(n, len(every)):
                            load_weights(every[issued])
                            issued += 1

                    load_up_to(2)
                    sp.dma_start(values[1][:, 0:MEM_T].rearrange("p a b c -> p a (b c)"),
                                 vm_dram[:, bass.ds(it, 1)].rearrange("t u p h n -> p (u t) (h n)")) \
                        .then_inc(mem_landed, 16)
                    sp.dma_start(KM, km_dram[bass.ds(it, 1)].rearrange("u p h s -> p (u h) s")) \
                        .then_inc(mem_landed, 16)
                    sp.dma_start(near_f[:, :], near_dram[bass.ds(it, 1)].rearrange("a p n -> (a p) n")) \
                        .then_inc(near_landed, 16)
                    for op, *args in plan.script:
                        if op == "convert":
                            load_up_to(args[0][0] + 3)
                        if op == "stacks":
                            t, c = args
                            at = slice(c * BANK, (c + 1) * BANK)
                            if t:
                                sp.wait_ge(s_full, plan.last_chunk[t - 1])
                            sp.wait_ge(j_free, last_group_job(t, c) + 1)
                            if not UNIT[t].has_k:
                                sp.dma_start(stack[:, 0:2, at], planes[:, HQ:LQ + 1, at]).then_inc(stacked[c], 16)
                                continue
                            for h in range(2):
                                src = planes[h * 64:h * 64 + 64, :, at]
                                dst = stack[:, 3 * h:3 * h + 3, at]
                                sp.dma_start(dst[0:64], src[:, 0:3, :]).then_inc(stacked[c], 16)
                                sp.dma_start(dst[64:128], src[:, 3:0:-1, :]).then_inc(stacked[c], 16)
                        if op == "sums":
                            sp.wait_ge(s_free, plan.last_chunk[STICK])
                            sp.dma_start(c_rows, c_dram[:, bass.ds(2 * it, 2), :]).then_inc(c_landed, 16)
                        if op == "store":
                            g = args[0]
                            yg = g // 4
                            t, i = plan.steps[g]
                            sp.wait_ge(j_free, plan.y_job[g][0] + 1)
                            dst = y_dram.rearrange("h (u f) s -> u f h s", f=P)
                            sp.dma_start(dst[bass.ds(UNIT[t].group * UNITS + it, 1), :, :,
                                             (i - 3) * P:(i + 1) * P].rearrange("u f h s -> (u f) h s"),
                                         y_halves[:, yg % 2]).then_inc(y_stored[yg % 2], STORE)
                    for b in range(2):
                        sp.wait_ge(y_stored[b], STORE * Y_GROUPS // 2)

                @block.tensor
                def _(pe):
                    def bank_of(j):
                        n = j[0]
                        if n >= J_BANKS:
                            pe.wait_ge(j_free, n - J_BANKS + 1)
                        return j_bank[n % J_BANKS]

                    def part(j, k0, k1):
                        n, what, t, kind, index = j
                        if k0 == 0:
                            unit = plan.steps[index][0] if what == "g" else t
                            if index == (unit * NT if what == "g" else 0) and (unit, kind) != (0, Q):
                                pe.wait_ge(w_ready, plan.conv_of[unit, kind] + 1)
                            bank_of(j)
                        bank = j_bank[n % J_BANKS]
                        if what == "qk":
                            dst = bank[:, :]
                            pairs = [(wt[:, kind, a, k, :], hT[:, b, k, index * BANK:(index + 1) * BANK])
                                     for k in range(k0, k1) for a, b in ((0, 0), (0, 1), (1, 0))]
                        else:
                            i = index if what == "v" else plan.steps[index][1]
                            dst = bank[:, 0:P]
                            pairs = [(hT[:, a, k, i * P:(i + 1) * P], wt[:, kind, b, k, :])
                                     for k in range(k0, k1) for a, b in ((0, 0), (0, 1), (1, 0))]
                        for q, (lhs, rhs) in enumerate(pairs):
                            last = nc.tensor.matmul(dst, lhs, rhs, start=(k0 == 0 and q == 0),
                                                    stop=(k1 == KT and q == len(pairs) - 1))
                        if k1 == KT:
                            last.then_inc(j_full, 1)

                    def scores(g, n, m, c, w):
                        t, i = plan.steps[g]
                        kind = KINDS[g]
                        if n == plan.chunks[g][0][0]:
                            if i % 4 == 0:
                                pe.wait_ge(stacked[i // 4], STACKED[t])
                            if kind == "forget" and i == 0:
                                pe.wait_ge(c_landed, 16)
                            if kind == "diff" and i == 0:
                                pe.wait_ge(near_step, 5)
                            if kind == "mem" and i == 0:
                                pe.wait_ge(mem_landed, 32)
                        if n >= S_BANKS:
                            pe.wait_ge(s_free, n - S_BANKS + 1)
                        bank = s_bank[n % S_BANKS]
                        parts = []
                        if kind == "mem":
                            for a, b in ((0, 0), (0, 1), (1, 0)):
                                parts.append((0, w, stack[:, a, i * P:(i + 1) * P], KM[:, b, :]))
                        else:
                            for a in (1, 2):
                                parts.append((0, w, stack[:, 3 * m + a, i * P:(i + 1) * P],
                                              stack[:, 3 * m, c:c + w]))
                        if kind == "forget":
                            parts.append((0, w, ones3[:, :], c_rows[:, m, c:c + w]))
                        if kind in ("stick", "forget") and c + w == (i + 1) * P:
                            parts.append((w - P, P, ident_b[:, :],
                                          (strict if kind == "stick" else causal)[:, :]))
                        if kind == "diff":
                            first = max(c, (i - 1) * P)
                            if first < c + w:
                                at, width = first - c, c + w - first
                                off = first - (i - 1) * P
                                for a in range(3):
                                    parts.append((at, width, ident_b[:, :], near[:, a, off:off + width]))
                        for q, (at, width, lhs, rhs) in enumerate(parts):
                            last = nc.tensor.matmul(bank[:, at:at + width], lhs, rhs, start=(q == 0),
                                                    stop=(q == len(parts) - 1), skip_group_check=True)
                        last.then_inc(s_full, 1)

                    def turn(g, tau, m, k0, tiles):
                        if KINDS[g] == "diff":
                            pe.wait_ge(combined, tau - DIFF_TAU + 1)
                        else:
                            pe.wait_ge(probs_ready, plan.chunk_at(g, m, k0) + 1)
                        if tau >= T_BANKS:
                            pe.wait_ge(t_free, tau - T_BANKS + 1)
                        for k in range(tiles):
                            last = nc.tensor.transpose(t_bank[tau % T_BANKS][:, k * P:(k + 1) * P],
                                                       row(g, m)[:, (k0 + k) * P:(k0 + k + 1) * P], ident[:, :])
                        last.then_inc(t_full, 1)

                    def mix(g, tau, m, k0, tiles, first, end):
                        unit = UNIT[plan.steps[g][0]]
                        if first and g:
                            pe.wait_ge(o_copied, g)
                        pe.wait_ge(t_free, tau + 1)
                        wide = P if KINDS[g] in ("diff", "mem") else HEAD_DIM
                        v = values[unit.slot]
                        for k in range(tiles):
                            for q, (a, b) in enumerate(((0, 0), (0, 1), (1, 0))):
                                last = nc.tensor.matmul(
                                    o_bank[:, m * HEAD_DIM:m * HEAD_DIM + wide],
                                    turned[:, tau % PT_RING, a, k * P:(k + 1) * P],
                                    v[:, k0 + k, b, m * HEAD_DIM:m * HEAD_DIM + wide],
                                    start=(first and k == 0 and q == 0), stop=(end and k == tiles - 1 and q == 2),
                                    skip_group_check=True)
                        last.then_inc(pv_done, 1)

                    for op, *args in plan.script:
                        if op == "part":
                            part(*args)
                        if op == "scores":
                            scores(args[0], *args[1])
                        if op == "turn":
                            turn(args[0], *args[1])
                        if op == "mix":
                            mix(args[0], *args[1], first=args[2], end=args[3])
                        if op == "y":
                            g = args[0]
                            bank = bank_of(plan.y_job[g])
                            pe.wait_ge(post_step, POST_AT[g] + POST[KINDS[g]])
                            nc.tensor.transpose(bank[:, 0:P], y_f[:, g % 2, :], ident[:, :]).then_inc(j_full, 1)

                @block.scalar
                def _(act):
                    def convert(c):
                        n, t, kind = c
                        act.wait_ge(w_in_sem[n % 2], (n // 2 + 1) * 16)
                        nc.scalar.activation(wt[:, kind, 0],
                                             ws[:, n % 2, :].rearrange("p (k n) -> p k n", k=KT), ACT.Copy,
                                             scale=W_SCALE).then_inc(w_hi, 1)

                    def high(j):
                        n, what, t, kind, index = j
                        src, dst, _, scale = job_out(j)
                        act.wait_ge(j_full, n + 1)
                        if what == "qk" and t:
                            act.wait_ge(stacked[index], STACKED[t - 1])
                        if what == "y" and index % 4 == 0:
                            yg = index // 4
                            act.wait_ge(y_stored[yg % 2], yg // 2 * STORE)
                        nc.scalar.activation(dst, src, ACT.Copy, scale=scale).then_inc(j_hi, 1)

                    def stick_exp(n, w):
                        e = e_buf[n % 3][:, 0:w]
                        act.wait_ge(s_full, n + 1)
                        at = n - plan.first_chunk[STICK]
                        nc.scalar.activation(e, s_bank[n % S_BANKS][:, 0:w], ACT.Abs).then_inc(stick_abs, 1)
                        act.wait_ge(stick_abs, at + 1)
                        nc.scalar.activation(e, e, ACT.Exp, scale=-1.0).then_inc(stick_e, 1)

                    def stick_log(n, w):
                        e = e_buf[n % 3][:, 0:w]
                        act.wait_ge(stick_e, n - plan.first_chunk[STICK] + 1)
                        nc.scalar.activation(e, e, ACT.Ln, bias=one[:, :]).then_inc(stick_ln, 1)

                    for op, *args in plan.script:
                        g = args[0]
                        if op == "convert":
                            convert(*args)
                        if op == "halves":
                            high(*args)
                        if op == "y":
                            high(plan.y_job[g])
                        if op == "scores" and KINDS[g] == "stick":
                            stick_exp(args[1][0], args[1][3])
                        if op == "log":
                            stick_log(args[1][0], args[1][3])
                        if op == "gate":
                            act.wait_ge(j_free, plan.gate_job[g][0] + 1)
                            nc.scalar.activation(gate_e[:, :], gate_f[:, :], ACT.Exp, scale=-1.0) \
                                .then_inc(j_hi, 1)
                        if op == "silu":
                            act.wait_ge(j_hi, plan.gate_job[g][0] + 1)
                            nc.scalar.activation(gate_e[:, :], gate_e[:, :], ACT.Ln, bias=one[:, :]) \
                                .then_inc(gate_ln, 1)
                            act.wait_ge(gate_ln, g + 1)
                            nc.scalar.activation(gate_e[:, :], gate_e[:, :], ACT.Exp, scale=-1.0) \
                                .then_inc(gate_exp, 1)
                        if op == "turn":
                            tau, m, k0, tiles = args[1]
                            w = tiles * P
                            act.wait_ge(t_full, tau + 1)
                            if tau >= PT_RING:
                                act.wait_ge(pv_done, tau - PT_RING + 1)
                            nc.scalar.copy(turned[:, tau % PT_RING, 0, 0:w], t_bank[tau % T_BANKS][:, 0:w]) \
                                .then_inc(t_hi, 1)
                        if op == "take":
                            act.wait_ge(pv_done, mixed(g))
                            if g:
                                act.wait_ge(post_step, POST_AT[g])
                            nc.scalar.copy(o_copy[:, :], o_bank[:, 0:P]).then_inc(o_copied, 1)
                        if op == "root":
                            d = DIFF_STEP[g]
                            act.wait_ge(var_ready, d + 1)
                            nc.scalar.activation(sc[:, 3:4], sc[:, 2:3], ACT.Ln).then_inc(var_ln, 1)
                            act.wait_ge(var_ln, d + 1)
                            nc.scalar.activation(sc[:, 4:5], sc[:, 3:4], ACT.Exp, scale=-0.5) \
                                .then_inc(root_done, 1)
                        if op == "exp":
                            n, m, c, w = args[1]
                            mine = row(g, m)[:, c:c + w]
                            if KINDS[g] == "stick":
                                act.wait_ge(s_free, n + 1)
                                nc.scalar.activation(mine, mine, ACT.Exp).then_inc(probs_ready, 1)
                            else:
                                act.wait_ge(max_ready, ROW_OF[g, m] + 1)
                                r = (2 * g + m) % ROWS
                                nc.scalar.activation(mine, mine, ACT.Exp, bias=neg_max[:, r:r + 1],
                                                     accum_out=z_part[:, r, c // BANK:c // BANK + 1]) \
                                    .then_inc(probs_ready, 1)

                @block.vector
                def _(dve):
                    def low(j):
                        n, what, t, kind, index = j
                        src, hi, lo, scale = job_out(j)
                        dve.wait_ge(j_hi, n + 1)
                        nc.vector.scalar_tensor_tensor(lo, src, scale, hi, op0=ALU.mult, op1=ALU.subtract) \
                            .then_inc(j_free, 1)

                    def convert(c):
                        n, t, kind = c
                        dve.wait_ge(w_hi, n + 1)
                        nc.vector.scalar_tensor_tensor(
                            wt[:, kind, 1], ws[:, n % 2, :].rearrange("p (k n) -> p k n", k=KT), W_SCALE,
                            wt[:, kind, 0], op0=ALU.mult, op1=ALU.subtract).then_inc(w_ready, 1)

                    def stick_chunk(g, n, m, c, w):
                        at = n - plan.first_chunk[STICK]
                        e, s, z = e_buf[n % 3][:, 0:w], c_buf[n % 2][:, 0:w], s_bank[n % S_BANKS][:, 0:w]
                        dve.wait_ge(stick_ln, at + 1)
                        nc.vector.scalar_tensor_tensor(e, z, 0.0, e, op0=ALU.max, op1=ALU.add) \
                            .then_inc(stick_sp, 1)
                        dve.wait_ge(stick_sp, at + 1)
                        first = c + w == (plan.steps[g][1] + 1) * P
                        if not first:
                            dve.wait_ge(stick_sum, at)
                        start = 0.0 if first else c_buf[(n - 1) % 2][:, 0:1]
                        nc.vector.tensor_tensor_scan(out=s[:, ::-1], data0=e[:, ::-1], data1=e[:, ::-1],
                                                     initial=start, op0=ALU.add, op1=ALU.bypass) \
                            .then_inc(stick_sum, 1)
                        dve.wait_ge(stick_sum, at + 1)
                        nc.vector.tensor_tensor(row(g, m)[:, c:c + w], z, s, ALU.subtract).then_inc(s_free, 1)

                    def soft_chunk(g, n, m, c, w):
                        r = (2 * g + m) % ROWS
                        dve.wait_ge(s_full, n + 1)
                        nc.vector.tensor_scalar(row(g, m)[:, c:c + w], s_bank[n % S_BANKS][:, 0:w], 1.0,
                                                -3.0e38, ALU.mult, ALU.max,
                                                accum_out=mx[:, r, c // BANK:c // BANK + 1]).then_inc(s_free, 1)

                    def row_max(g, m):
                        mine = [ch for ch in plan.chunks[g] if ch[1] == m]
                        r = (2 * g + m) % ROWS
                        dve.wait_ge(s_free, mine[-1][0] + 1)
                        nc.vector.tensor_reduce(neg_max[:, r:r + 1], mx[:, r, 0:len(mine)], AX_X, ALU.max,
                                                negate=True).then_inc(max_ready, 1)

                    def sum_rows(g, heads):
                        r, cuts = 2 * g % ROWS, len([ch for ch in plan.chunks[g] if ch[1] == 0])
                        return nc.vector.tensor_reduce(z_sum[:, r:r + heads], z_part[:, r:r + heads, 0:cuts], AX_X,
                                                       ALU.add)

                    def combine(g, tau, m, k0, tiles):
                        at = DIFF_STEP[g] * COEF
                        if k0 == 0:
                            z0, z1 = z_sum[:, col(g, 0)], z_sum[:, col(g, 1)]
                            dve.wait_ge(probs_ready, plan.last_of(g, 1) + 1)
                            sum_rows(g, 2).then_inc(coef_step, 1)
                            dve.wait_ge(coef_step, at + 1)
                            nc.vector.reciprocal(sc[:, 0:1], z1).then_inc(coef_step, 1)
                            dve.wait_ge(coef_step, at + 2)
                            nc.vector.tensor_tensor(sc[:, 0:1], sc[:, 0:1], z0, ALU.mult).then_inc(coef_step, 1)
                            dve.wait_ge(coef_step, at + 3)
                            nc.vector.tensor_tensor(sc[:, 1:2], sc[:, 0:1], neg_lam[:, :], ALU.mult) \
                                .then_inc(coef_step, 1)
                            dve.wait_ge(coef_step, at + 4)
                        s = slice(k0 * P, (k0 + tiles) * P)
                        nc.vector.scalar_tensor_tensor(row(g, 0)[:, s], row(g, 1)[:, s], sc[:, 1:2],
                                                       row(g, 0)[:, s], op0=ALU.mult, op1=ALU.add) \
                            .then_inc(combined, 1)

                    def take_gate(g):
                        dve.wait_ge(j_full, plan.gate_job[g][0] + 1)
                        if g:
                            dve.wait_ge(gate_done, g)
                        nc.vector.tensor_scalar(gate_f[:, :], job_out(plan.gate_job[g])[0], 1.0 / W_SCALE,
                                                GATE_MIN, ALU.mult, ALU.max).then_inc(j_free, 1)

                    def silu(g):
                        if g:
                            dve.wait_ge(post_step, POST_AT[g])
                        dve.wait_ge(gate_exp, g + 1)
                        nc.vector.tensor_tensor(gate_s[:, :], gate_f[:, :], gate_e[:, :], ALU.mult) \
                            .then_inc(gate_done, 1)

                    def variance(g):
                        at = POST_AT[g]
                        rz0 = rz[:, 0:1]
                        nc.vector.reciprocal(rz0, z_sum[:, col(g, 0)]).then_inc(post_step, 1)
                        dve.wait_ge(o_copied, g + 1)
                        nc.vector.tensor_tensor_reduce(out=junk[:, :], in0=o_copy[:, :], in1=o_copy[:, :],
                                                       scale=1.0, scalar=0.0, op0=ALU.mult, op1=ALU.add,
                                                       accum_out=sc[:, 6:7]).then_inc(post_step, 1)
                        dve.wait_ge(gate_done, g + 1)
                        nc.vector.tensor_tensor(gate_s[:, :], gate_s[:, :], head_gain[:, :], ALU.mult) \
                            .then_inc(post_step, 1)
                        dve.wait_ge(post_step, at + 3)
                        nc.vector.tensor_scalar(sc[:, 7:8], sc[:, 6:7], rz0, rz0, ALU.mult, ALU.mult) \
                            .then_inc(post_step, 1)
                        dve.wait_ge(post_step, at + 4)
                        nc.vector.tensor_scalar(sc[:, 2:3], sc[:, 7:8], 1.0 / P, EPS, ALU.mult, ALU.add) \
                            .then_inc(var_ready, 1)

                    def post(g):
                        kind = KINDS[g]
                        at = POST_AT[g]
                        y = y_f[:, g % 2, :]
                        if g >= 2:
                            dve.wait_ge(j_full, plan.y_job[g - 2][0] + 1)
                        dve.wait_ge(gate_done, g + 1)
                        if kind == "stick":
                            dve.wait_ge(o_copied, g + 1)
                            nc.vector.tensor_tensor(y, o_copy[:, :], gate_s[:, :], ALU.mult).then_inc(post_step, 1)
                        elif kind in ("forget", "mem"):
                            heads = 2 if kind == "forget" else 1
                            wide = P // heads
                            r = 2 * g % ROWS
                            dve.wait_ge(o_copied, g + 1)
                            sum_rows(g, heads).then_inc(post_step, 1)
                            dve.wait_ge(post_step, at + 1)
                            nc.vector.reciprocal(rz[:, 0:heads], z_sum[:, r:r + heads]).then_inc(post_step, 1)
                            dve.wait_ge(post_step, at + 2)
                            for h in range(heads):
                                s = slice(h * wide, (h + 1) * wide)
                                last = nc.vector.scalar_tensor_tensor(y[:, s], o_copy[:, s], rz[:, h:h + 1],
                                                                      gate_s[:, s], op0=ALU.mult, op1=ALU.mult)
                            last.then_inc(post_step, 1)
                        else:
                            v, r0, h, rz0 = sc[:, 2:3], sc[:, 4:5], sc[:, 5:6], rz[:, 0:1]
                            dve.wait_ge(root_done, DIFF_STEP[g] + 1)
                            nc.vector.tensor_scalar(h, v, r0, r0, ALU.mult, ALU.mult).then_inc(post_step, 1)
                            dve.wait_ge(post_step, at + 5)
                            nc.vector.tensor_scalar(h, h, -0.5, 1.5, ALU.mult, ALU.add).then_inc(post_step, 1)
                            dve.wait_ge(post_step, at + 6)
                            nc.vector.tensor_tensor(h, h, r0, ALU.mult).then_inc(post_step, 1)
                            dve.wait_ge(post_step, at + 7)
                            nc.vector.tensor_tensor(h, h, rz0, ALU.mult).then_inc(post_step, 1)
                            dve.wait_ge(post_step, at + 8)
                            nc.vector.scalar_tensor_tensor(y, o_copy[:, :], h, gate_s[:, :], op0=ALU.mult,
                                                           op1=ALU.mult).then_inc(post_step, 1)

                    def split_near():
                        dve.wait_ge(near_landed, 16)
                        for a in range(3):
                            nc.vector.tensor_copy(near[:, a, :], near_f[:, ::-1]).then_inc(near_step, 1)
                            if a < 2:
                                dve.wait_ge(near_step, 2 * a + 1)
                                nc.vector.tensor_tensor(near_f[:, :], near_f[:, :], near[:, a, ::-1], ALU.subtract) \
                                    .then_inc(near_step, 1)
                                dve.wait_ge(near_step, 2 * a + 2)

                    for op, *args in plan.script:
                        g = args[0]
                        if op == "convert":
                            convert(*args)
                        if op == "halves":
                            low(*args)
                        if op == "y":
                            low(plan.y_job[g])
                        if op == "scores" and KINDS[g] != "stick":
                            if KINDS[g] == "diff" and args[1][0] == plan.first_chunk[plan.steps[g][0]]:
                                split_near()
                            soft_chunk(g, *args[1])
                        if op == "log":
                            stick_chunk(g, *args[1])
                        if op == "peak":
                            row_max(g, args[1])
                        if op == "combine":
                            combine(g, *args[1])
                        if op == "turn":
                            tau, m, k0, tiles = args[1]
                            w = tiles * P
                            dve.wait_ge(t_hi, tau + 1)
                            nc.vector.tensor_tensor(turned[:, tau % PT_RING, 1, 0:w],
                                                    t_bank[tau % T_BANKS][:, 0:w],
                                                    turned[:, tau % PT_RING, 0, 0:w], ALU.subtract) \
                                .then_inc(t_free, 1)
                        if op == "gate":
                            take_gate(g)
                        if op == "silu":
                            silu(g)
                        if op == "variance":
                            variance(g)
                        if op == "post":
                            post(g)
            with nc.Block() as block:
                @block.gpsimd
                def _(pool):
                    for s in loop_sems:
                        nc.gpsimd.sem_clear(s)

        PAIRS = NT // 2
        yl = [rows_flat[:, b * YT * 2 * P:(b + 1) * YT * 2 * P].bitcast(F16)
              .rearrange("p (h k s) -> p h k s", h=2, k=YT) for b in range(2)]
        flat = stack_flat[:, 0:5 * 2 * D].bitcast(F32)
        x_res = [flat[:, b * D:(b + 1) * D] for b in range(2)]
        o_out = [flat[:, (2 + b) * D:(3 + b) * D] for b in range(2)]
        gain_out = flat[:, 4 * D:5 * D]
        out_banks = [(s_bank[0], s_bank[1]), (t_bank[0], t_bank[1])]
        scrap = [j_bank[0], j_bank[1]]
        wo_in, y_in, x_in2, out_stored = ([sem(f"{n}{b}") for b in range(2)]
                                          for n in ("wo_landed", "y_landed", "res_landed", "out_stored"))
        wo_hi, wo_ready, gain_in, out_full, out_sq, out_root, out_step, out_ready = (
            sem(n) for n in ("wo_hi", "wo_ready", "gain_landed", "out_full", "out_sq", "out_root", "out_step",
                             "out_ready"))
        var_sum = sem("var_sum")
        OUT_STEPS = 6
        with nc.Block() as block:
            @block.sync
            def _(sp):
                def load_y(q):
                    if q >= 2:
                        sp.wait_ge(out_full, 2 * (q - 1))
                    src = y_dram[:, :, q * 2 * P:(q + 1) * 2 * P].rearrange("h (k f) s -> f h k s", f=P)
                    for h in range(2):
                        sp.dma_start(yl[q % 2][:, h], src[:, h]).then_inc(y_in[q % 2], 16)

                for k in range(YT):
                    if k >= 2:
                        sp.wait_ge(wo_ready, k - 1)
                    if k == 0:
                        load_y(0)
                    sp.dma_start(ws[:, k % 2, :], w_out_rows[k]).then_inc(wo_in[k % 2], 16)
                    if k == 9:
                        load_y(1)
                        sp.dma_start(gain_out, post_norm[0].partition_broadcast(P)).then_inc(gain_in, 16)
                for i in range(NT):
                    if i >= 2:
                        sp.wait_ge(out_ready, i - 1)
                    sp.dma_start(x_res[i % 2], x[0, i * P:(i + 1) * P, :]).then_inc(x_in2[i % 2], 16)
                    if i >= 1:
                        sp.wait_ge(out_ready, i)
                        sp.dma_start(out[0, (i - 1) * P:i * P, :], o_out[(i - 1) % 2]) \
                            .then_inc(out_stored[(i - 1) % 2], 16)
                    if i % 2 == 0 and i // 2 + 1 >= 2 and i // 2 + 1 < PAIRS:
                        load_y(i // 2 + 1)
                sp.wait_ge(out_ready, NT)
                sp.dma_start(out[0, (NT - 1) * P:NT * P, :], o_out[(NT - 1) % 2]) \
                    .then_inc(out_stored[(NT - 1) % 2], 16)
                for b in range(2):
                    sp.wait_ge(out_stored[b], 16 * (NT // 2))

            @block.tensor
            def _(pe):
                pe.wait_ge(y_in[0], 32)
                for k in range(YT):
                    pe.wait_ge(wo_ready, k + 1)
                    for i in range(2):
                        for n in range(2):
                            for a, b in ((0, 0), (0, 1), (1, 0)):
                                last = nc.tensor.matmul(
                                    out_banks[i][n][:, :], yl[0][:, a, k, i * P:(i + 1) * P],
                                    wo[:, b, k, n * BANK:(n + 1) * BANK], start=(k == 0 and a == b == 0),
                                    stop=(k == YT - 1 and a == 1))
                        if k == YT - 1:
                            last.then_inc(out_full, 1)
                for i in range(2, NT):
                    if i % 2 == 0:
                        pe.wait_ge(y_in[i // 2 % 2], 32 * (i // 4 + 1))
                    pe.wait_ge(out_step, OUT_STEPS * (i - 1))
                    y = yl[i // 2 % 2]
                    for n in range(2):
                        for k in range(YT):
                            for a, b in ((0, 0), (0, 1), (1, 0)):
                                last = nc.tensor.matmul(
                                    out_banks[i % 2][n][:, :], y[:, a, k, (i % 2) * P:(i % 2 + 1) * P],
                                    wo[:, b, k, n * BANK:(n + 1) * BANK], start=(k == 0 and a == b == 0),
                                    stop=(k == YT - 1 and a == 1))
                    last.then_inc(out_full, 1)

            @block.scalar
            def _(act):
                for k in range(YT):
                    act.wait_ge(wo_in[k % 2], 16 * (k // 2 + 1))
                    nc.scalar.activation(wo[:, 0, k], ws[:, k % 2, :], ACT.Copy, scale=W_SCALE).then_inc(wo_hi, 1)
                for i in range(NT):
                    act.wait_ge(out_full, i + 1)
                    for n in range(2):
                        nc.scalar.activation(scrap[n][:, :], out_banks[i % 2][n][:, :], ACT.Square,
                                             scale=1.0 / W_SCALE, accum_out=sc[:, n:n + 1]).then_inc(out_sq, 1)
                    act.wait_ge(out_step, OUT_STEPS * i + 1)
                    nc.scalar.activation(sc[:, 3:4], sc[:, 2:3], ACT.Ln).then_inc(out_root, 1)
                    act.wait_ge(out_root, 2 * i + 1)
                    nc.scalar.activation(sc[:, 4:5], sc[:, 3:4], ACT.Exp, scale=-0.5).then_inc(out_root, 1)

            @block.vector
            def _(dve):
                for k in range(YT):
                    dve.wait_ge(wo_hi, k + 1)
                    nc.vector.scalar_tensor_tensor(wo[:, 1, k], ws[:, k % 2, :], W_SCALE, wo[:, 0, k],
                                                   op0=ALU.mult, op1=ALU.subtract).then_inc(wo_ready, 1)
                dve.wait_ge(gain_in, 16)
                for i in range(NT):
                    v, r0, h = sc[:, 2:3], sc[:, 4:5], sc[:, 5:6]
                    at = OUT_STEPS * i
                    dve.wait_ge(out_sq, 2 * i + 2)
                    nc.vector.tensor_tensor(sc[:, 6:7], sc[:, 0:1], sc[:, 1:2], ALU.add).then_inc(var_sum, 1)
                    dve.wait_ge(var_sum, i + 1)
                    nc.vector.tensor_scalar(v, sc[:, 6:7], 1.0 / D, EPS, ALU.mult, ALU.add).then_inc(out_step, 1)
                    dve.wait_ge(out_root, 2 * i + 2)
                    nc.vector.tensor_scalar(h, v, r0, r0, ALU.mult, ALU.mult).then_inc(out_step, 1)
                    dve.wait_ge(out_step, at + 2)
                    nc.vector.tensor_scalar(h, h, -0.5 / W_SCALE, 1.5 / W_SCALE, ALU.mult, ALU.add) \
                        .then_inc(out_step, 1)
                    dve.wait_ge(out_step, at + 3)
                    nc.vector.tensor_tensor(h, h, r0, ALU.mult).then_inc(out_step, 1)
                    dve.wait_ge(out_step, at + 4)
                    if i >= 2:
                        dve.wait_ge(out_stored[i % 2], 16 * (i // 2))
                    for n in range(2):
                        s = slice(n * BANK, (n + 1) * BANK)
                        nc.vector.scalar_tensor_tensor(o_out[i % 2][:, s], out_banks[i % 2][n][:, :], h,
                                                       gain_out[:, s], op0=ALU.mult, op1=ALU.mult) \
                            .then_inc(out_step, 1)
                    dve.wait_ge(out_step, at + 6)
                    dve.wait_ge(x_in2[i % 2], 16 * (i // 2 + 1))
                    nc.vector.tensor_tensor(o_out[i % 2], o_out[i % 2], x_res[i % 2], ALU.add) \
                        .then_inc(out_ready, 1)


NAMES = ["x", "mem", "w_in", "b_forget", "w_mem_kv", "w_out", "pre_norm", "post_norm", "mem_norm",
         "diff_lambda", "diff_head_norm", "rel_bias"]


def kernel(**inputs):
    import concourse.bacc as bacc
    from concourse.bass_utils import run_bass_kernel_spmd

    nc = bacc.Bacc("TRN2", target_bir_lowering=False, num_devices=1)
    arrays = {name: np.ascontiguousarray(inputs[name]) for name in NAMES}
    arrays["pick"], arrays["dmask"] = distance_tables(3 * P)
    args = [nc.dram_tensor(name, a.shape, mybir.dt.from_np(a.dtype), kind="ExternalInput").ap()
            for name, a in arrays.items()]
    shape = arrays["x"].shape
    args.append(nc.dram_tensor("out", shape, F32, kind="ExternalOutput").ap())
    build(nc, *args)
    result = run_bass_kernel_spmd(nc, [arrays], core_ids=[0])
    return result.results[0]["out"]
```
